# Optimizing a Trainium2 kernel written in Bass

```python
import jax, jax.numpy as jnp
from jax import lax
import numpy as np
import math

D_MODEL = 2048
BATCH = 1
SEQ = 256
DEPTH = 1

D_A = D_MODEL // 2
HEAD_SIZE = 64
N_HEADS_A = D_A // HEAD_SIZE
LORA_W = 64
LORA_A = 64
D_B = D_MODEL // 2
CONV_GROUPS = 16
CONV_WIDTH = 3
N_BRANCH = 2
RMS_EPS = 1e-6
GN_EPS = 64e-5

COLS_A = 3 * D_A + LORA_W + LORA_A
OFF_ZA = COLS_A
OFF_B = OFF_ZA + D_A
OFF_GATE = OFF_B + 4 * D_B
N_IN = OFF_GATE + N_BRANCH * D_MODEL


def rms_norm(x, g):
    xf = x.astype(jnp.float32)
    y = xf * lax.rsqrt(jnp.mean(xf * xf, axis=-1, keepdims=True) + RMS_EPS)
    return (y * g.astype(jnp.float32)).astype(x.dtype)

def shift_time(u, n):
    return jnp.pad(u, ((0, 0), (n, 0), (0, 0)))[:, : u.shape[1]]

def wkv7_scan(r, decay, k, v, kk, b):
    def step(S, inp):
        r_t, w_t, k_t, v_t, kk_t, b_t = inp
        sa = jnp.einsum('bhvk,bhk->bhv', S, -kk_t)
        S = (S * w_t[:, :, None, :]
             + sa[..., None] * b_t[:, :, None, :]
             + v_t[..., None] * k_t[:, :, None, :])
        y_t = jnp.einsum('bhvk,bhk->bhv', S, r_t)
        return S, y_t
    xs = (jnp.swapaxes(r, 0, 1), jnp.swapaxes(decay, 0, 1), jnp.swapaxes(k, 0, 1),
          jnp.swapaxes(v, 0, 1), jnp.swapaxes(kk, 0, 1), jnp.swapaxes(b, 0, 1))
    bsz, _, nh, n = r.shape
    S0 = jnp.zeros((bsz, nh, n, n), jnp.float32)
    _, y = lax.scan(step, S0, xs)
    return jnp.swapaxes(y, 0, 1)

def rwkv7_mix(pa, w0, w2, a0, a2, k_k, k_a, r_k, lnx_g, lnx_b):
    bsz, t, _ = pa.shape
    pa = pa.astype(jnp.float32)
    r = pa[..., :D_A]
    k = pa[..., D_A:2 * D_A]
    v = pa[..., 2 * D_A:3 * D_A]
    xw = pa[..., 3 * D_A:3 * D_A + LORA_W]
    xa = pa[..., 3 * D_A + LORA_W:]
    f = lambda p: p.astype(jnp.float32)
    w_log = -jax.nn.softplus(-(f(w0) + jnp.tanh(xw) @ f(w2))) - 0.5
    decay = jnp.exp(-jnp.exp(w_log))
    a = jax.nn.sigmoid(f(a0) + xa @ f(a2))
    hs = (bsz, t, N_HEADS_A, HEAD_SIZE)
    kk = (k * f(k_k)).reshape(hs)
    kk = kk / jnp.maximum(jnp.sqrt(jnp.sum(kk * kk, axis=-1, keepdims=True)), 1e-12)
    k = k * (1.0 + (a - 1.0) * f(k_a))
    r_h, k_h, v_h = r.reshape(hs), k.reshape(hs), v.reshape(hs)
    b_h = kk * a.reshape(hs)
    y = wkv7_scan(r_h, decay.reshape(hs), k_h, v_h, kk, b_h)
    mu = jnp.mean(y, axis=-1, keepdims=True)
    var = jnp.mean(jnp.square(y - mu), axis=-1, keepdims=True)
    y = ((y - mu) * lax.rsqrt(var + GN_EPS)).reshape(bsz, t, D_A) * f(lnx_g) + f(lnx_b)
    bonus = jnp.sum(r_h * k_h * f(r_k), axis=-1, keepdims=True) * v_h
    return y + bonus.reshape(bsz, t, D_A)

def short_conv_mix(pb, conv_w):
    bg = pb[..., :D_B]
    cg = pb[..., D_B:2 * D_B]
    hb = pb[..., 2 * D_B:]
    u = cg * hb
    y = conv_w[0] * shift_time(u, 2) + conv_w[1] * shift_time(u, 1) + conv_w[2] * u
    return bg * y

def first_inputs(seed: int = 0) -> dict:
    key = jax.random.key(seed)
    ks = jax.random.split(key, 24)
    L, D = DEPTH, D_MODEL
    nrm = lambda k, s, sc: jax.random.normal(k, s, jnp.float32) * sc
    return {
        "x": nrm(ks[0], (BATCH, SEQ, D), 1.0),
        "c": nrm(ks[1], (BATCH, D), 1.0),
        "ada_w": nrm(ks[2], (L, D, 3 * D), 0.5 * D ** -0.5),
        "ada_b": nrm(ks[3], (L, 3 * D), 0.01),
        "pre_gain": 1.0 + nrm(ks[4], (L, D), 0.05),
        "post_gain": 1.0 + nrm(ks[5], (L, D), 0.05),
        "w_in": nrm(ks[6], (L, D, N_IN), D ** -0.5),
        "mu_shift": jax.random.uniform(ks[7], (L, COLS_A), jnp.float32),
        "w0": nrm(ks[8], (L, D_A), 1.0),
        "w2": nrm(ks[9], (L, LORA_W, D_A), 0.5 * LORA_W ** -0.5),
        "a0": nrm(ks[10], (L, D_A), 0.5),
        "a2": nrm(ks[11], (L, LORA_A, D_A), 0.5 * LORA_A ** -0.5),
        "k_k": 0.85 + nrm(ks[12], (L, D_A), 0.05),
        "k_a": 1.0 + nrm(ks[13], (L, D_A), 0.05),
        "r_k": nrm(ks[14], (L, N_HEADS_A, HEAD_SIZE), 0.1),
        "lnx_gain": 1.0 + nrm(ks[15], (L, D_A), 0.05),
        "lnx_bias": nrm(ks[16], (L, D_A), 0.01),
        "conv_w": nrm(ks[17], (L, CONV_WIDTH, D_B), CONV_WIDTH ** -0.5),
        "p_a": nrm(ks[18], (L, D_A, D), D_A ** -0.5),
        "p_b": nrm(ks[19], (L, D_B, D), D_B ** -0.5),
        "w_out": nrm(ks[20], (L, D, D), D ** -0.5),
    }

def first_block(x, c, ada_w, ada_b, pre_gain, post_gain, w_in, mu_shift, w0, w2, a0, a2,
              k_k, k_a, r_k, lnx_gain, lnx_bias, conv_w, p_a, p_b, w_out):
    D = D_MODEL
    c_act = jax.nn.silu(c)
    for l in range(DEPTH):
        mod = c_act @ ada_w[l] + ada_b[l]
        shift = mod[:, None, :D]
        scale = mod[:, None, D:2 * D]
        gate = mod[:, None, 2 * D:]
        h = rms_norm(x, pre_gain[l]) * (1.0 + scale) + shift
        proj = h @ w_in[l]
        pa = proj[..., :COLS_A]
        pa = pa + (shift_time(pa, 1) - pa) * mu_shift[l]
        z_a = proj[..., OFF_ZA:OFF_B]
        pb = proj[..., OFF_B:OFF_B + 3 * D_B]
        z_b = proj[..., OFF_B + 3 * D_B:OFF_GATE]
        g_a = proj[..., OFF_GATE:OFF_GATE + D]
        g_b = proj[..., OFF_GATE + D:]
        y_a = rwkv7_mix(pa, w0[l], w2[l], a0[l], a2[l], k_k[l], k_a[l], r_k[l],
                        lnx_gain[l], lnx_bias[l]).astype(x.dtype)
        y_a = (y_a * jax.nn.silu(z_a)) @ p_a[l]
        y_b = (short_conv_mix(pb, conv_w[l]) * jax.nn.silu(z_b)) @ p_b[l]
        m = jax.nn.sigmoid(g_a) * y_a + jax.nn.sigmoid(g_b) * y_b
        o = m @ w_out[l]
        x = x + gate * rms_norm(o, post_gain[l])
    return x


N_MIXERS = 3
D_FF = 4 * D_MODEL
D_PLE = 256
NORM_EPS = 1e-6
LN_EPS = 1e-5
NEG = -1e30

NSA_HEADS = 16
NSA_KV_HEADS = 4
NSA_HPG = NSA_HEADS // NSA_KV_HEADS
NSA_HEAD_DIM = D_MODEL // NSA_HEADS
NSA_CMP_LEN = 32
NSA_CMP_STRIDE = 16
NSA_CMP_HIDDEN = NSA_HEAD_DIM
NSA_SEL_LEN = 64
NSA_SEL_TOPK = 16
NSA_SEL_LOCAL = 2
NSA_WINDOW = 512
NSA_Q_BLOCK = 32
NSA_FORCE = 1e9
NSA_IN_WIDTH = NSA_HEADS * NSA_HEAD_DIM + 6 * NSA_KV_HEADS * NSA_HEAD_DIM + 3 * NSA_HEADS

CONV_WIDTH_2 = 31
CONV_INNER = D_MODEL

GLA_HEADS = 4
GLA_DK = D_MODEL // 2 // GLA_HEADS
GLA_DV = D_MODEL // GLA_HEADS
GLA_GATE_RANK = 16
GLA_GATE_NORM = 16.0
GLA_CHUNK = 64
GLA_IN_WIDTH = 2 * GLA_HEADS * GLA_DK + 2 * GLA_HEADS * GLA_DV + GLA_GATE_RANK


def rms_norm_2(x, gain):
    xf = x.astype(jnp.float32)
    y = xf * lax.rsqrt(jnp.mean(xf * xf, axis=-1, keepdims=True) + NORM_EPS)
    return (y * gain.astype(jnp.float32)).astype(x.dtype)

def layer_norm(x, gain, bias):
    xf = x.astype(jnp.float32)
    mu = jnp.mean(xf, axis=-1, keepdims=True)
    xc = xf - mu
    y = xc * lax.rsqrt(jnp.mean(xc * xc, axis=-1, keepdims=True) + LN_EPS)
    return (y * gain.astype(jnp.float32) + bias.astype(jnp.float32)).astype(x.dtype)

def masked_softmax(s, valid):
    s = jnp.where(valid, s.astype(jnp.float32), NEG)
    return jax.nn.softmax(s, axis=-1) * valid

def nsa_mixer(h, w_in, w_out, pos_k, w1_k, w2_k, pos_v, w1_v, w2_v):
    B, S, _ = h.shape
    G, HPG, Dh = NSA_KV_HEADS, NSA_HPG, NSA_HEAD_DIM
    kvw = G * Dh
    proj = h @ w_in
    cuts = [NSA_HEADS * Dh + i * kvw for i in range(7)]
    q, kc, vc, ks, vs, kw, vw, gates = jnp.split(proj, cuts, axis=-1)
    q = q.reshape(B, S, G, HPG, Dh) * (Dh ** -0.5)
    kc, vc, ks, vs, kw, vw = (a.reshape(B, S, G, Dh) for a in (kc, vc, ks, vs, kw, vw))
    gates = jax.nn.sigmoid(gates.reshape(B, S, G, HPG, 3))

    n_cmp = (S - NSA_CMP_LEN) // NSA_CMP_STRIDE + 1
    cmp_idx = np.arange(n_cmp)[:, None] * NSA_CMP_STRIDE + np.arange(NSA_CMP_LEN)[None, :]
    cmp_end = cmp_idx[:, -1]

    def compress(kv, pos, w1, w2):
        blk = kv[:, cmp_idx] + pos[None, None, :, None, :]
        blk = blk.transpose(0, 1, 3, 2, 4).reshape(B, n_cmp, G, NSA_CMP_LEN * Dh)
        return jax.nn.silu(blk @ w1) @ w2

    k_cmp = compress(kc, pos_k, w1_k, w2_k)
    v_cmp = compress(vc, pos_v, w1_v, w2_v)

    n_sel = S // NSA_SEL_LEN
    n_top = min(NSA_SEL_TOPK, n_sel)
    cmp_start = np.arange(n_cmp) * NSA_CMP_STRIDE
    sel_start = np.arange(n_sel) * NSA_SEL_LEN
    overlap = jnp.asarray(((cmp_start[:, None] <= sel_start[None, :] + NSA_SEL_LEN - 1)
                           & (cmp_start[:, None] + NSA_CMP_LEN - 1 >= sel_start[None, :])).astype(np.float32))
    ks_blk = ks.reshape(B, n_sel, NSA_SEL_LEN, G, Dh).transpose(0, 3, 1, 2, 4)
    vs_blk = vs.reshape(B, n_sel, NSA_SEL_LEN, G, Dh).transpose(0, 3, 1, 2, 4)
    b_ix = jnp.arange(B)[:, None, None, None]
    g_ix = jnp.arange(G)[None, :, None, None]
    blk_ids = jnp.arange(n_sel)
    tok_off = jnp.arange(NSA_SEL_LEN)

    pad = ((0, 0), (NSA_WINDOW, 0), (0, 0), (0, 0))
    kw_pad = jnp.pad(kw, pad)
    vw_pad = jnp.pad(vw, pad)
    QB = NSA_Q_BLOCK

    def block(start):
        t = start + jnp.arange(QB)
        qb = lax.dynamic_slice_in_dim(q, start, QB, axis=1)
        gb = lax.dynamic_slice_in_dim(gates, start, QB, axis=1)

        valid_c = cmp_end[None, :] <= t[:, None]
        p_c = masked_softmax(jnp.einsum('bqghd,bngd->bghqn', qb, k_cmp), valid_c)
        o_c = jnp.einsum('bghqn,bngd->bqghd', p_c.astype(v_cmp.dtype), v_cmp)

        imp = jnp.einsum('bghqn,nm->bgqm', p_c, overlap)
        diff = (t // NSA_SEL_LEN)[:, None] - blk_ids[None, :]
        forced = (blk_ids[None, :] == 0) | ((diff >= 0) & (diff < NSA_SEL_LOCAL))
        imp = jnp.where(forced, NSA_FORCE, imp)
        imp = jnp.where(diff >= 0, imp, -NSA_FORCE)
        _, sel = lax.top_k(imp, n_top)
        k_sel = ks_blk[b_ix, g_ix, sel]
        v_sel = vs_blk[b_ix, g_ix, sel]
        tok = sel[..., None] * NSA_SEL_LEN + tok_off
        valid_s = (tok <= t[None, None, :, None, None]).reshape(B, G, 1, QB, n_top * NSA_SEL_LEN)
        s_s = jnp.einsum('bqghd,bgqnld->bghqnl', qb, k_sel).reshape(B, G, HPG, QB, n_top * NSA_SEL_LEN)
        p_s = masked_softmax(s_s, valid_s)
        o_s = jnp.einsum('bghqk,bgqkd->bqghd', p_s.astype(v_sel.dtype),
                         v_sel.reshape(B, G, QB, n_top * NSA_SEL_LEN, Dh))

        kwb = lax.dynamic_slice_in_dim(kw_pad, start, QB + NSA_WINDOW, axis=1)
        vwb = lax.dynamic_slice_in_dim(vw_pad, start, QB + NSA_WINDOW, axis=1)
        kpos = start - NSA_WINDOW + jnp.arange(QB + NSA_WINDOW)
        valid_w = ((kpos[None, :] <= t[:, None]) & (kpos[None, :] > t[:, None] - NSA_WINDOW)
                   & (kpos[None, :] >= 0))
        p_w = masked_softmax(jnp.einsum('bqghd,bkgd->bghqk', qb, kwb), valid_w)
        o_w = jnp.einsum('bghqk,bkgd->bqghd', p_w.astype(vwb.dtype), vwb)

        return gb[..., 0, None] * o_c + gb[..., 1, None] * o_s + gb[..., 2, None] * o_w

    out = lax.map(block, jnp.arange(S // QB) * QB)
    out = out.transpose(1, 0, 2, 3, 4, 5).reshape(B, S, NSA_HEADS * Dh)
    return out @ w_out

def conv_mixer(h, w_in, dw, db, ln_g, ln_b, w_out):
    a, g = jnp.split(h @ w_in, 2, axis=-1)
    u = a * jax.nn.sigmoid(g)
    y = lax.conv_general_dilated(
        u, dw[:, None, :], window_strides=(1,), padding=[(CONV_WIDTH_2 - 1, 0)],
        dimension_numbers=('NWC', 'WIO', 'NWC'), feature_group_count=CONV_INNER) + db
    y = jax.nn.silu(layer_norm(y, ln_g, ln_b))
    return y @ w_out

def gla_mixer(h, w_in, w_gate_up, b_gate, norm_g, w_out):
    B, S, _ = h.shape
    H, dk, dv, C = GLA_HEADS, GLA_DK, GLA_DV, GLA_CHUNK
    nC = S // C
    cuts = [H * dk, 2 * H * dk, 2 * H * dk + H * dv, 2 * H * dk + 2 * H * dv]
    q, k, v, r, gz = jnp.split(h @ w_in, cuts, axis=-1)
    glog = jax.nn.log_sigmoid((gz @ w_gate_up + b_gate).astype(jnp.float32)) / GLA_GATE_NORM
    f32 = jnp.float32
    q = q.astype(f32).reshape(B, nC, C, H, dk) * (dk ** -0.5)
    k = k.astype(f32).reshape(B, nC, C, H, dk)
    v = v.astype(f32).reshape(B, nC, C, H, dv)
    bcum = jnp.cumsum(glog.reshape(B, nC, C, H, dk), axis=2)
    blast = bcum[:, :, -1]
    q_dec = q * jnp.exp(bcum)
    k_intra = k * jnp.exp(-bcum)
    k_state = k * jnp.exp(blast[:, :, None] - bcum)
    causal = jnp.asarray(np.tril(np.ones((C, C), dtype=bool)))
    A = jnp.where(causal, jnp.einsum('bncha,bnsha->bnhcs', q_dec, k_intra), 0.0)
    o_intra = jnp.einsum('bnhcs,bnshv->bnchv', A, v)

    def step(state, xs):
        qd, kst, vv, dl = xs
        o = jnp.einsum('bcha,bhav->bchv', qd, state)
        state = state * jnp.exp(dl)[..., None] + jnp.einsum('bcha,bchv->bhav', kst, vv)
        return state, o

    xs = tuple(jnp.moveaxis(a, 1, 0) for a in (q_dec, k_state, v, blast))
    _, o_inter = lax.scan(step, jnp.zeros((B, H, dk, dv), f32), xs)
    o = (o_intra + jnp.moveaxis(o_inter, 0, 1)).reshape(B, S, H, dv)
    o = o * lax.rsqrt(jnp.mean(o * o, axis=-1, keepdims=True) + NORM_EPS) * norm_g.astype(f32)
    o = o.reshape(B, S, H * dv).astype(h.dtype) * jax.nn.silu(r)
    return o @ w_out

def second_inputs(seed: int = 0) -> dict:
    key = jax.random.key(seed)
    keys = iter(jax.random.split(key, 64))

    def nrm(shape, scale):
        return jax.random.normal(next(keys), shape, jnp.float32) * scale

    def gain(shape):
        return 1.0 + nrm(shape, 0.02)

    n_nsa = len(range(0, DEPTH, N_MIXERS))
    n_conv = len(range(1, DEPTH, N_MIXERS))
    n_gla = len(range(2, DEPTH, N_MIXERS))
    D, Dh, L = D_MODEL, NSA_HEAD_DIM, NSA_CMP_LEN
    return {
        "x": nrm((BATCH, SEQ, D), 1.0),
        "p": nrm((DEPTH, BATCH, SEQ, D_PLE), 1.0),
        "norm_mix": gain((DEPTH, D)),
        "norm_ffn": gain((DEPTH, D)),
        "norm_ple": gain((DEPTH, D)),
        "norm_final": gain((D,)),
        "ffn_w1": nrm((DEPTH, D, D_FF), D ** -0.5),
        "ffn_w2": nrm((DEPTH, D_FF, D), D_FF ** -0.5),
        "ple_w_proj": nrm((DEPTH, D_PLE, D), D_PLE ** -0.5),
        "ple_w_gate": nrm((DEPTH, D, D), D ** -0.5),
        "nsa_w_in": nrm((n_nsa, D, NSA_IN_WIDTH), D ** -0.5),
        "nsa_w_out": nrm((n_nsa, NSA_HEADS * Dh, D), (NSA_HEADS * Dh) ** -0.5),
        "nsa_cmp_pos_k": nrm((n_nsa, L, Dh), 0.02),
        "nsa_cmp_w1_k": nrm((n_nsa, L * Dh, NSA_CMP_HIDDEN), (L * Dh) ** -0.5),
        "nsa_cmp_w2_k": nrm((n_nsa, NSA_CMP_HIDDEN, Dh), NSA_CMP_HIDDEN ** -0.5),
        "nsa_cmp_pos_v": nrm((n_nsa, L, Dh), 0.02),
        "nsa_cmp_w1_v": nrm((n_nsa, L * Dh, NSA_CMP_HIDDEN), (L * Dh) ** -0.5),
        "nsa_cmp_w2_v": nrm((n_nsa, NSA_CMP_HIDDEN, Dh), NSA_CMP_HIDDEN ** -0.5),
        "conv_w_in": nrm((n_conv, D, 2 * CONV_INNER), D ** -0.5),
        "conv_dw": nrm((n_conv, CONV_WIDTH_2, CONV_INNER), CONV_WIDTH_2 ** -0.5),
        "conv_db": nrm((n_conv, CONV_INNER), 0.01),
        "conv_ln_g": gain((n_conv, CONV_INNER)),
        "conv_ln_b": nrm((n_conv, CONV_INNER), 0.01),
        "conv_w_out": nrm((n_conv, CONV_INNER, D), CONV_INNER ** -0.5),
        "gla_w_in": nrm((n_gla, D, GLA_IN_WIDTH), D ** -0.5),
        "gla_w_gate_up": nrm((n_gla, GLA_GATE_RANK, GLA_HEADS * GLA_DK), GLA_GATE_RANK ** -0.5),
        "gla_b_gate": nrm((n_gla, GLA_HEADS * GLA_DK), 0.01),
        "gla_norm_g": gain((n_gla, GLA_DV)),
        "gla_w_out": nrm((n_gla, GLA_HEADS * GLA_DV, D), (GLA_HEADS * GLA_DV) ** -0.5),
    }

def second_block(x, p, norm_mix, norm_ffn, norm_ple, norm_final, ffn_w1, ffn_w2,
              ple_w_proj, ple_w_gate, nsa_w_in, nsa_w_out, nsa_cmp_pos_k, nsa_cmp_w1_k,
              nsa_cmp_w2_k, nsa_cmp_pos_v, nsa_cmp_w1_v, nsa_cmp_w2_v, conv_w_in, conv_dw,
              conv_db, conv_ln_g, conv_ln_b, conv_w_out, gla_w_in, gla_w_gate_up,
              gla_b_gate, gla_norm_g, gla_w_out):
    h = x
    for i in range(DEPTH):
        m, j = i % N_MIXERS, i // N_MIXERS
        hn = rms_norm_2(h, norm_mix[i])
        if m == 0:
            y = nsa_mixer(hn, nsa_w_in[j], nsa_w_out[j], nsa_cmp_pos_k[j], nsa_cmp_w1_k[j],
                          nsa_cmp_w2_k[j], nsa_cmp_pos_v[j], nsa_cmp_w1_v[j], nsa_cmp_w2_v[j])
        elif m == 1:
            y = conv_mixer(hn, conv_w_in[j], conv_dw[j], conv_db[j], conv_ln_g[j],
                           conv_ln_b[j], conv_w_out[j])
        else:
            y = gla_mixer(hn, gla_w_in[j], gla_w_gate_up[j], gla_b_gate[j], gla_norm_g[j],
                          gla_w_out[j])
        h = h + y
        hn = rms_norm_2(h, norm_ffn[i])
        h = h + jnp.square(jax.nn.relu(hn @ ffn_w1[i])) @ ffn_w2[i]
        gate = jax.nn.sigmoid(rms_norm_2(h, norm_ple[i]) @ ple_w_gate[i])
        h = h + (p[i] @ ple_w_proj[i]) * gate
    return rms_norm_2(h, norm_final)


def setup_inputs(seed=0):
    out = dict(first_inputs(seed))
    for name, value in second_inputs(seed + 1).items():
        if name != "x":
            out[name + "_2"] = value
    return out


def reference(
    x, c, ada_w, ada_b, pre_gain, post_gain, w_in, mu_shift, w0, w2, a0, a2, k_k, k_a, r_k,
    lnx_gain, lnx_bias, conv_w, p_a, p_b, w_out, p_2, norm_mix_2, norm_ffn_2, norm_ple_2,
    norm_final_2, ffn_w1_2, ffn_w2_2, ple_w_proj_2, ple_w_gate_2, nsa_w_in_2, nsa_w_out_2,
    nsa_cmp_pos_k_2, nsa_cmp_w1_k_2, nsa_cmp_w2_k_2, nsa_cmp_pos_v_2, nsa_cmp_w1_v_2,
    nsa_cmp_w2_v_2, conv_w_in_2, conv_dw_2, conv_db_2, conv_ln_g_2, conv_ln_b_2, conv_w_out_2,
    gla_w_in_2, gla_w_gate_up_2, gla_b_gate_2, gla_norm_g_2, gla_w_out_2,
):
    x = first_block(
        x, c, ada_w, ada_b, pre_gain, post_gain, w_in, mu_shift, w0, w2, a0, a2, k_k, k_a, r_k,
        lnx_gain, lnx_bias, conv_w, p_a, p_b, w_out,
    )
    return second_block(
        x, p_2, norm_mix_2, norm_ffn_2, norm_ple_2, norm_final_2, ffn_w1_2, ffn_w2_2,
        ple_w_proj_2, ple_w_gate_2, nsa_w_in_2, nsa_w_out_2, nsa_cmp_pos_k_2, nsa_cmp_w1_k_2,
        nsa_cmp_w2_k_2, nsa_cmp_pos_v_2, nsa_cmp_w1_v_2, nsa_cmp_w2_v_2, conv_w_in_2, conv_dw_2,
        conv_db_2, conv_ln_g_2, conv_ln_b_2, conv_w_out_2, gla_w_in_2, gla_w_gate_up_2,
        gla_b_gate_2, gla_norm_g_2, gla_w_out_2,
    )


_drawn_inputs = setup_inputs


def setup_inputs(seed=0):
    import zlib

    import numpy as np

    out = dict(_drawn_inputs(seed))
    spreads = {}
    factors = {'ada_b': 4.147,
     'post_gain': 3.482,
     'w2': 3.762,
     'k_k': 8.0,
     'k_a': 4.328,
     'lnx_gain': 6.109,
     'lnx_bias': 8.0,
     'norm_mix_2': 8.0,
     'norm_ffn_2': 9.558,
     'norm_ple_2': 200.0,
     'norm_final_2': 23.884,
     'nsa_cmp_pos_k_2': 8.0,
     'nsa_cmp_pos_v_2': 43.409,
     'p_2': 8.0,
     'ple_w_proj_2': 8.0,
     'ple_w_gate_2': 8.0}
    for name, (base, spread) in spreads.items():
        noise = np.random.default_rng([zlib.crc32(name.encode()), seed]).standard_normal(out[name].shape)
        drawn = base * np.exp(spread * noise) if base else spread * noise
        out[name] = __import__('jax').numpy.asarray(drawn.astype(out[name].dtype))
    for name, factor in factors.items():
        out[name] = (out[name] * factor).astype(out[name].dtype)
    return out
```

```python
from contextlib import ExitStack

import numpy as np

import concourse.bass as bass
from concourse import mybir

P = 128
T = 256
D = 2048
KT = D // P
DA = D // 2
HT = DA // P
HS = 64
CH = 64
NC = T // CH
LORA = 64
DFF = 4 * D
QH, GQ, HPG = 16, 4, 4
DH = 128
CL, CS = 32, 16
NCMP = (T - CL) // CS + 1
NP32 = 32
DPLE = 256
GCOL = 64
NEG = -1e30
EPS = 1e-6
GN_EPS = 64e-5
EXP_M_HALF = float(np.exp(-0.5))

F32 = mybir.dt.float32
F32R = mybir.dt.float32r
ACT = mybir.ActivationFunctionType
ALU = mybir.AluOpType
AX_X = mybir.AxisListType.X

RAW, SPLIT = 8, 4
CW = 1024
AHEAD = 3
ADA0 = 0
WA0 = ADA0 + 2 * D // CW * KT
XW0 = WA0 + 8 * 8
WB0 = XW0 + 2
PAB0 = WB0 + 16 * 8
WO0 = PAB0 + 4 * 8
NS0 = WO0 + 4 * 8
GT0 = NS0 + 10 * 8
CM0 = GT0 + 1
NO0 = CM0 + 8
FF0 = NO0 + 4 * 8
PR0 = FF0 + 4 * 64
PG0 = PR0 + 4
END = PG0 + 4 * 8

NG = 10
G_KS, G_VS, G_KW, G_VW, G_KC, G_VC = range(4, 10)
LAST = END

DVE_STEPS = 30
ATTN_STEPS = 26
HPV = 10
V_HP = 0
V_CONV = V_HP + HT * HPV
V_MUX = V_CONV + 3 * HT
V_PRE = V_MUX + 1
V_POST = V_PRE + KT
V_MIX = V_POST + KT
V_FFN = V_MIX + KT
V_PLE = V_FFN + KT
V_FIN = V_PLE + KT
V_C = V_FIN + KT
V_ADAB = V_C + KT
V_POSK = V_ADAB + 3 * KT
V_POSV = V_POSK + CL
NVEC = V_POSV + CL

C_ID = 0
C_G = C_ID + P
C_UP = C_G + 4 * P
C_BLK = C_UP + 6 * P
C_BLKM = C_BLK + P
C_ONE = C_BLKM + P
C_CAU = C_ONE + P
C_VAL = C_CAU + P
C_NEG = C_VAL + 2 * NP32
NCON = C_NEG + 2 * NP32


def shape_constants():
    c = np.zeros((P, NCON), np.float32)
    i, j = np.arange(P)[:, None], np.arange(P)[None, :]
    c[:, C_ID:C_ID + P] = i == j
    for n, m in enumerate((j > i, j >= i) * 2):
        c[:, C_G + n * P:C_G + (n + 1) * P] = m
    for n in range(6):
        b = 2 ** n
        c[:, C_UP + n * P:C_UP + (n + 1) * P] = (i // (2 * b) == j // (2 * b)) & (i // b % 2 == 0) & (j // b % 2 == 1)
    c[:, C_BLK:C_BLK + P] = i // HS == j // HS
    c[:, C_BLKM:C_BLKM + P] = (i // HS == j // HS) / HS
    c[:, C_ONE:C_ONE + P] = 1
    c[:, C_CAU:C_CAU + P] = np.where(j <= i, 0, NEG)
    n = np.arange(NP32)[None, :]
    for q in range(2):
        ok = (n * CS + CL - 1 <= q * P + i) & (n < NCMP)
        c[:, C_VAL + q * NP32:C_VAL + (q + 1) * NP32] = ok
        c[:, C_NEG + q * NP32:C_NEG + (q + 1) * NP32] = np.where(ok, 0, NEG)
    return c


def blocks(w):
    k, n = w.shape
    return w.reshape(k // 256, 2, P, n // 512, 512).transpose(3, 0, 2, 1, 4).reshape(-1, P, CW)


def columns(v):
    return v.reshape(-1, P).T


def lay_out(i):
    w_in = i["w_in"][0]
    tile = lambda a: w_in[:, a:a + P]
    za, bg = 3 * DA + 2 * LORA, 4 * DA + 2 * LORA
    cg, hb, zb, ga = bg + DA, bg + 2 * DA, bg + 3 * DA, bg + 4 * DA
    conv_and_gates = []
    for h in range(HT):
        conv_and_gates += [tile(s + h * P) for s in (cg, hb, bg, zb)]
        conv_and_gates += [tile(ga + (4 * h + n) * P) for n in range(4)]
    nsa = i["nsa_w_in_2"][0]
    by_group = []
    for g in range(GQ):
        by_group.append(nsa[:, g * HPG * DH:(g + 1) * HPG * DH])
        by_group += [nsa[:, D + n * GQ * DH + g * DH:][:, :DH] for n in (2, 3, 4, 5, 0, 1)]
    gates = np.pad(nsa[:, D + 6 * GQ * DH:], ((0, 0), (0, GCOL - 3 * QH)))
    p_ab = [np.concatenate([i[p][0][:, b * 512:(b + 1) * 512] for p in ("p_b", "p_a")], 0) for b in range(4)]
    w1, w2 = i["ffn_w1_2"][0], i["ffn_w2_2"][0]
    ada = i["ada_w"][0].reshape(KT, P, 6, CW).transpose(2, 0, 1, 3).reshape(-1, P, CW)
    stream = [
        ada[:WA0],
        blocks(np.concatenate([w_in[:, :3 * DA], w_in[:, za:bg]], 1)),
        w_in[:, 3 * DA:za].reshape(2, 8, P, P).transpose(0, 2, 1, 3).reshape(2, P, CW),
        blocks(np.concatenate(conv_and_gates, 1)),
        *[blocks(p) for p in p_ab],
        blocks(i["w_out"][0]),
        blocks(np.concatenate(by_group, 1)),
        gates.reshape(KT, P, GCOL).transpose(1, 0, 2).reshape(1, P, CW),
        *[i[w][0].reshape(4, 8, P, P).transpose(0, 2, 1, 3).reshape(4, P, CW)
          for w in ("nsa_cmp_w1_k_2", "nsa_cmp_w1_v_2")],
        blocks(i["nsa_w_out_2"][0]),
    ]
    for f in range(4):
        stream += [blocks(w1[:, f * D:(f + 1) * D]), blocks(w2[f * D:(f + 1) * D])]
    stream += [blocks(i["ple_w_proj_2"][0]), blocks(i["ple_w_gate_2"][0])]
    stream = np.concatenate(stream, 0)
    assert stream.shape == (END, P, CW), stream.shape

    mu = i["mu_shift"][0]
    pairs = [mu[:DA], mu[DA:2 * DA], mu[2 * DA:3 * DA]] + [i[n][0].reshape(-1) for n in (
        "w0", "a0", "k_k", "k_a", "r_k", "lnx_gain", "lnx_bias")]
    vec = np.concatenate(
        [np.stack([columns(v) for v in pairs], 2).reshape(P, -1),
         np.stack([columns(v) for v in i["conv_w"][0]], 2).reshape(P, -1),
         columns(mu[3 * DA:])]
        + [columns(i[n].reshape(-1)) for n in (
            "pre_gain", "post_gain", "norm_mix_2", "norm_ffn_2", "norm_ple_2", "norm_final_2", "c", "ada_b",
            "nsa_cmp_pos_k_2", "nsa_cmp_pos_v_2")], 1)
    assert vec.shape == (P, NVEC)
    channels_first = lambda x: x.T.reshape(-1, P, T).transpose(1, 0, 2)
    return {
        "stream": stream,
        "ada_gate": ada[WA0:],
        "vec": vec,
        "con": shape_constants(),
        "x": channels_first(i["x"][0]),
        "ple": channels_first(i["p_2"][0, 0]),
        "lora": np.concatenate([i["w2"][0], i["a2"][0]], 0),
        "cmp2": np.concatenate([i["nsa_cmp_w2_k_2"][0], i["nsa_cmp_w2_v_2"][0]], 1),
    }


class Steps:

    def __init__(self, eng, sem):
        self.eng, self.sem, self.base, self.n, self.i, self.per = eng, sem, 0, 0, None, 0

    def do(self, ins):
        ins.then_inc(self.sem, 1)
        self.n += 1

    def wait(self):
        v = self.base + self.n
        self.eng.wait_ge(self.sem, v if self.i is None else self.i * self.per + v)

    def step(self, ins):
        self.do(ins)
        self.wait()

    def enter(self, i, per):
        self.base, self.n, self.i, self.per = self.base + self.n, 0, i, per

    def leave(self, count):
        assert self.n == self.per, (self.n, self.per)
        self.base, self.n, self.i = self.base + self.per * count, 0, None


def block_of_two_layers(nc, stream, ada_gate, vec_in, con_in, x_in, ple_in, lora_in, cmp2_in, out):
    ctx = ExitStack()
    with ctx:
        base = (nc.sbuf_base + 63) // 64 * 64

        def sb(name, shape, at, dt=F32):
            size = 4 * int(np.prod(shape[1:]))
            assert base + at + size <= nc.sbuf_usable_end, (name, at + size)
            t = nc.alloc_sbuf_tensor_at(name, shape, dt, offset=base + at)
            return t, (at + size + 31) // 32 * 32

        def sem(name):
            return ctx.enter_context(nc.semaphore(name))

        raw, o = sb("raw", [P, RAW, CW], 0)
        whi, o = sb("whi", [P, SPLIT, CW], o, F32R)
        wlo, o = sb("wlo", [P, SPLIT, CW], o, F32R)
        acts, o = sb("acts", [P, KT, 2 * T], o, F32R)
        con, o = sb("con", [P, NCON], o)
        vec, o = sb("vec", [P, NVEC], o)
        mod, o = sb("mod", [P, 3 * KT], o)
        gpre, o = sb("gpre", [P, KT], o)
        gpost, o = sb("gpost", [P, KT], o)
        cact, o = sb("cact", [P, KT], o)
        rs, o = sb("rs", [P, T], o)
        epsc, o = sb("epsc", [P, 2], o)
        rst, o = sb("rst", [P, 2], o)
        cg, o = sb("cg", [P, 4], o)
        spare, o = sb("spare", [P, 1], o)
        half, o = sb("half", [P, 4, T], o)
        xt, free = sb("xt", [P, KT, T], o)
        acc, _ = sb("acc", [P, 2 * D], free)
        scr0, _ = sb("scr0", [P, KT, T], free + 24 * 1024)
        r_, a = sb("r_", [P, HT, T + 1], free)
        k_, a = sb("k_", [P, HT, T + 1], a)
        v_, a = sb("v_", [P, HT, T + 1], a)
        za, a = sb("za", [P, HT, T], a)
        xz, wkv0 = sb("xz", [P, 2 * T], a)
        ar, a = sb("ar", [P, NC, 4 * CH], o)
        gm, a = sb("gm", [P, NC, 4 * P], a)
        kk, a = sb("kk", [P, T], a)
        kp, a = sb("kp", [P, T], a)
        rm, a = sb("rm", [P, T], a)
        km, a = sb("km", [P, T], a)
        assert a <= free
        graw, _ = sb("graw", [P, 4, CW], o)
        gacc, _ = sb("gacc", [P, D], wkv0 + 4 * (T + 3 * NC * P))
        vm, a = sb("vm", [P, T], wkv0)
        bx, a = sb("bx", [P, NC, P], a)
        kx, a = sb("kx", [P, NC, P], a)
        vx, a = sb("vx", [P, NC, P], a)
        mi, a = sb("mi", [P, NC, P], a)
        mt, a = sb("mt", [P, NC, P], a)
        lt, a = sb("lt", [P, NC, P], a)
        ts, a = sb("ts", [P, NC, P], a)
        st, a = sb("st", [P, 2, P], a)
        sa, a = sb("sa", [P, 2, P], a)
        hv, a = sb("hv", [P, HPV], a)
        lw, a = sb("lw", [P, P], a)
        ca, a = sb("ca", [P, NC, 32 + CH], a)
        cb, a = sb("cb", [P, NC, 32 + CH], a)
        aa, a = sb("aa", [P, T], a)
        pw, a = sb("pw", [P, T], a)
        pp, a = sb("pp", [P, T], a)
        pi, a = sb("pi", [P, T], a)
        t1, a = sb("t1", [P, T], a)
        t2, a = sb("t2", [P, T], a)
        sw, a = sb("sw", [P, T], a)
        stage, a = sb("stage", [P, 8, T], a)
        cu, a = sb("cu", [P, T + 2], a)
        cy, a = sb("cy", [P, T], a)
        cz, a = sb("cz", [P, T], a)
        hc, a = sb("hc", [P, 3], a)
        rm2, a = sb("rm2", [P, T], a)
        lora, a = sb("lora", [P, DA], a)
        yab, a = sb("yab", [P, 2, HT, 2 * T], wkv0, F32R)
        gab, a = sb("gab", [P, 2, 4, T], free + 3 * 4 * HT * (T + 1))
        ob, a = sb("ob", [P, KT, T], free)
        sqa, a = sb("sqa", [P, 4, T], wkv0)
        sqt, a = sb("sqt", [P, 4, T], a)
        m4, a = sb("m4", [P, 4, T], free + 2 * 4 * HT * (T + 1))
        m5, a = sb("m5", [P, 4, T], a)

        nsb, a = sb("nsb", [P, GQ * NG, T], free)
        blkf, a2 = sb("blkf", [P, CL, GQ * NCMP], a)
        blks, _ = sb("blks", [P, CL, 2 * GQ * NCMP], a2, F32R)
        ng, a = sb("ng", [P, 8, T], a)
        pr1, a = sb("pr1", [P, HPG, 2 * T], a)
        pr0, a = sb("pr0", [P, HPG, T], a)
        hid, h = sb("hid", [P, 3, GQ * NCMP], a + 7 * 1024)
        hrep, _ = sb("hrep", [P, GQ, P], h)
        pt, a = sb("pt", [P, 5, 4 * P], a)
        vtm, a = sb("vtm", [P, 4, P], a)
        kcmp, a = sb("kcmp", [P, GQ, NP32], a)
        vcmp, a = sb("vcmp", [P, GQ, P], a)
        kcg, a = sb("kcg", [P, NP32], a)
        vcg, a = sb("vcg", [P, P], a)
        gt, a = sb("gt", [P, 2, GCOL], a)
        gg, a = sb("gg", [P, 2, 3 * HPG], a)
        pc, a = sb("pc", [P, 2 * HPG, NP32], a)
        mx, a = sb("mx", [P, 3, 2 * HPG], a)
        su, a = sb("su", [P, 3, 2 * HPG], a)
        nm, a = sb("nm", [P, 2, 2 * HPG], a)
        cmp2, a = sb("cmp2", [P, 2 * P], a)
        hff, _ = sb("hff", [P, KT, 2 * T], free, F32R)
        pj, a = sb("pj", [P, KT, T], free)
        y_, a = sb("y_", [P, KT, T], a)
        pe_, a = sb("pe_", [P, 2, T], a)
        pes, _ = sb("pes", [P, 2, 2 * T], a, F32R)
        s4, a = sb("s4", [P, 4, T], free + 64 * 1024)
        q4, a = sb("q4", [P, 4, T], a)
        sqb, a = sb("sqb", [P, 4, T], free + 48 * 1024)
        squ, a = sb("squ", [P, 4, T], a)

        gate_dram = nc.dram_tensor("gate_dram", (32, P, T), F32).ap()

        ps = [ctx.enter_context(nc.psum_tensor(f"ps{n}", [P, 512], F32)) for n in range(8)]

        raw_ready = [sem(f"raw_ready{n}") for n in range(RAW)]
        gate_in = [sem(f"gate_in{n}") for n in range(4)]
        raw_used = sem("raw_used")
        hi_done = sem("hi_done")
        quarters = sem("quarters")
        half_done = sem("half_done")
        evac_done = sem("evac_done")
        class s:
            loaded = sem("loaded")
            y_out = sem("y_out")
            out_done = sem("out_done")
            ss_ps = sem("ss_ps")
            pool_step = sem("pool_step")
            sq_sum = sem("sq_sum")
            eps_set = sem("eps_set")
            acts_ready = sem("acts_ready")
            gate_used = sem("gate_used")
            init_done = sem("init_done")
            ar_zero = sem("ar_zero")
            pool_moved = sem("pool_moved")
            yab_done = sem("yab_done")
            x_again = sem("x_again")
            mul_done = sem("mul_done")
            gab_in = sem("gab_in")
            x_done1 = sem("x_done1")
            cmp2_in = sem("cmp2_in")
            pads_set = sem("pads_set")
            blk_done = sem("blk_done")
            vcmp_done = sem("vcmp_done")
            attn_done = sem("attn_done")
            ple_in = sem("ple_in")
            res_done = sem("res_done")
            ple_done = sem("ple_done")
            rms_done = sem("rms_done")
            acts_hi = sem("acts_hi")
            cact_s = sem("cact_s")
            sq_done = sem("sq_done")
            h_done = sem("h_done")
            xz_mixed = sem("xz_mixed")
            xz_done = sem("xz_done")
            zb_sig = sem("zb_sig")
            vec_ready = sem("vec_ready")
            z_ps = sem("z_ps")
            gates_done = sem("gates_done")
            cum_ready = sem("cum_ready")
            exps_done = sem("exps_done")
            kn_in = sem("kn_in")
            root_done = sem("root_done")
            mixed = sem("mixed")
            vx_done = sem("vx_done")
            m_ps = sem("m_ps")
            m_first = sem("m_first")
            tr_ps = sem("tr_ps")
            tr_done = sem("tr_done")
            t_ps = sem("t_ps")
            t_done = sem("t_done")
            w_ps = sem("w_ps")
            w_done = sem("w_done")
            x_ps = sem("x_ps")
            x_done = sem("x_done")
            u2_ps = sem("u2_ps")
            u2_done = sem("u2_done")
            var_ps = sem("var_ps")
            ya_done = sem("ya_done")
            conv_done = sem("conv_done")
            yab_hi = sem("yab_hi")
            gab_sig = sem("gab_sig")
            m_sum = sem("m_sum")
            m_hi = sem("m_hi")
            rst_done = sem("rst_done")
            gt_done = sem("gt_done")
            blk_f = sem("blk_f")
            blk_hi = sem("blk_hi")
            hid_half = sem("hid_half")
            hid_sum = sem("hid_sum")
            hid_sig = sem("hid_sig")
            scaled = sem("scaled")
            ng_done = sem("ng_done")
            v_ps = sem("v_ps")
            vtm_done = sem("vtm_done")
            max_done = sem("max_done")
            exp_done = sem("exp_done")
            cd_done = sem("cd_done")
            cexp_done = sem("cexp_done")
            p_ps = sem("p_ps")
            pt_act = sem("pt_act")
            o_ps = sem("o_ps")
            o_hi = sem("o_hi")
            pes_hi = sem("pes_hi")
            relu_done = sem("relu_done")
            relu_hi = sem("relu_hi")
            pg_sig = sem("pg_sig")
            dve_step = sem("dve_step")
            rs_ready = sem("rs_ready")
            mod_ps = sem("mod_ps")
            cg_done = sem("cg_done")
            gate_ps = sem("gate_ps")
            lora_ready = sem("lora_ready")
            sq_ready = sem("sq_ready")
            ss2_ps = sem("ss2_ps")
            br_ready = sem("br_ready")
            ops_done = sem("ops_done")
            bs_ps = sem("bs_ps")
            bon_done = sem("bon_done")
            g_ps = sem("g_ps")
            gm_done = sem("gm_done")
            mt_upd = sem("mt_upd")
            lt_ready = sem("lt_ready")
            bk_scaled = sem("bk_scaled")
            u_ps = sem("u_ps")
            m_upd = sem("m_upd")
            ut_ps = sem("ut_ps")
            d_ps = sem("d_ps")
            s_done = sem("s_done")
            sa_ps = sem("sa_ps")
            sa_done = sem("sa_done")
            y_ps = sem("y_ps")
            yc_done = sem("yc_done")
            mu_ps = sem("mu_ps")
            ysq_done = sem("ysq_done")
            m_done = sem("m_done")
            rst_ps = sem("rst_ps")
            blk_lo = sem("blk_lo")
            hrep_done = sem("hrep_done")
            cmp_ps = sem("cmp_ps")
            kcmp_done = sem("kcmp_done")
            ng_dve = sem("ng_dve")
            s_ps = sem("s_ps")
            pr_done = sem("pr_done")
            pt_dve = sem("pt_dve")
            pes_lo = sem("pes_lo")
            relu_rs = sem("relu_rs")
            relu_lo = sem("relu_lo")
            pg_mul = sem("pg_mul")

        def tri(n):
            c = C_UP + n * P
            return con[:, c:c + P].rearrange("p (a n) -> p a n", a=1).to_broadcast([P, NC, P])

        ident = con[:, C_ID:C_ID + P]
        ident4 = ident.rearrange("p (a n) -> p a n", a=1).to_broadcast([P, NC, P])
        blk, blkm, ones = (con[:, c:c + P] for c in (C_BLK, C_BLKM, C_ONE))

        def each(t):
            return t[:, :].rearrange("p (c t) -> p c t", c=NC)

        def four(b):
            return ps[b][:, :].rearrange("p (c n) -> p c n", c=NC)

        def one(t):
            return t.rearrange("p a t -> p (a t)")

        def tile_of(t, i, lo=0, hi=T):
            return one(t[:, bass.ds(i, 1), lo:hi])

        heads = ((0, HS), (HS, P))
        block = ctx.enter_context(nc.Block())

        @block.sync
        def _(sp):
            sp.dma_start(vec[:, :], vec_in).then_inc(s.loaded, 16)
            sp.dma_start(con[:, :], con_in).then_inc(s.loaded, 16)
            sp.dma_start(xt[:, :, :], x_in).then_inc(s.loaded, 16)

            def load(g, i=0):
                sp.wait_ge(raw_used, i * RAW + (g + 1))
                sp.dma_start(raw[:, g % RAW, :], stream[bass.ds(i * RAW + g, 1), :, :].rearrange("a p n -> (a p) n")
                             ).then_inc(raw_ready[g % RAW], 16)

            with sp.Fori(0, LAST // RAW) as i:
                for g in range(RAW):
                    load(g, i)
            for g in range(LAST // RAW * RAW, LAST):
                load(g)
            for q in range(4):
                sp.wait_ge(s.y_out, q + 1)
                sp.dma_start(out[:, 4 * q:4 * q + 4, :], y_[:, 4 * q:4 * q + 4, :]).then_inc(s.out_done, 16)
            sp.wait_ge(s.out_done, 64)

        @block.gpsimd
        def _(gp):
            def squares(ready, first, src, use, sq_a, sq_t):
                gp.wait_ge(s.ss_ps, use)
                for q in range(4):
                    v = src[:, 4 * q:4 * q + 4, :]
                    gp.wait_ge(ready, first[q])
                    nc.gpsimd.tensor_tensor((sq_t if q else sq_a)[:, :, :], v, v, ALU.mult).then_inc(s.pool_step, 1)
                    if q:
                        gp.wait_ge(s.pool_step, 9 * (use - 1) + 2 * q)
                        nc.gpsimd.tensor_tensor(sq_a[:, :, :], sq_a[:, :, :], sq_t[:, :, :], ALU.add).then_inc(s.pool_step, 1)
                        gp.wait_ge(s.pool_step, 9 * (use - 1) + 2 * q + 1)
                nc.gpsimd.tensor_tensor(sq_a[:, 0:2, :], sq_a[:, 0:2, :], sq_a[:, 2:4, :], ALU.add).then_inc(s.pool_step, 2)
                gp.wait_ge(s.pool_step, 9 * use)
                nc.gpsimd.tensor_tensor(sq_a[:, 0, :], sq_a[:, 0, :], sq_a[:, 1, :], ALU.add).then_inc(s.sq_sum, 1)

            nc.gpsimd.memset(epsc[:, 0:1], EPS).then_inc(s.eps_set, 1)
            nc.gpsimd.memset(epsc[:, 1:2], GN_EPS).then_inc(s.eps_set, 1)
            nc.gpsimd.memset(half[:, 0, 0:1], 0.0).then_inc(raw_used, RAW)
            nc.gpsimd.memset(half[:, 1, 0:1], 0.0).then_inc(quarters, 4 * SPLIT)
            gp.wait_ge(s.acts_ready, KT)
            nc.gpsimd.memset(gacc[:, :], 0.0).then_inc(s.gate_used, 4)
            for t in (bx, kx, vx, ca, cb):
                nc.gpsimd.memset(t[:, :, :], 0.0).then_inc(s.init_done, 1)
            nc.gpsimd.memset(cu[:, :], 0.0).then_inc(s.init_done, 1)
            for t in (r_, k_, v_):
                nc.gpsimd.memset(t[:, :, 0:1], 0.0).then_inc(s.init_done, 1)
            nc.gpsimd.memset(xz[:, :], 0.0).then_inc(s.init_done, 1)
            with gp.Fori(0, 8) as i:
                for m in range(4):
                    gp.wait_ge(s.gate_used, i * 4 + (m + 1))
                    gp.dma_start(graw[:, m, :], ada_gate[bass.ds(i * 4 + m, 1), :, :].rearrange("a p n -> (a p) n")
                                 ).then_inc(gate_in[m], 16)
            gp.wait_ge(s.gate_used, 36)
            nc.gpsimd.memset(ar[:, :, :], 0.0).then_inc(s.ar_zero, 1)
            gp.dma_start(lora[:, :], lora_in).then_inc(s.pool_moved, 16)

            with gp.Fori(0, HT) as i:
                for n in range(4):
                    gp.wait_ge(evac_done, i * 8 + (38 + n))
                    gp.dma_start(gate_dram[bass.ds(i * 4 + n, 1), :, :].rearrange("a p t -> (a p) t"), stage[:, 4 + n, :]
                                 ).then_inc(s.pool_moved, 16)
            gp.wait_ge(s.pool_moved, 64 * HT + 16)
            gp.wait_ge(s.yab_done, 2 * HT)
            gp.dma_start(xt[:, :, :], x_in).then_inc(s.x_again, 16)
            for b in range(4):
                if b:
                    gp.wait_ge(s.mul_done, 8 * b)
                for n in range(2):
                    gp.dma_start(gab[:, n, :, :],
                                 gate_dram[KT * (1 - n) + 4 * b:KT * (1 - n) + 4 * b + 4, :, :].rearrange("a p t -> p a t")
                                 ).then_inc(s.gab_in, 16)
            squares(evac_done, [33 + 8 * HT + 32 + 4 * (q + 1) for q in range(4)], ob, 1, sqa, sqt)
            squares(s.x_done1, [1, 2, 3, 4], xt, 2, sqb, squ)
            gp.wait_ge(s.ss_ps, 3)
            gp.dma_start(cmp2[:, :], cmp2_in).then_inc(s.cmp2_in, 16)
            nc.gpsimd.memset(kcmp[:, :, :], 0.0).then_inc(s.pads_set, 1)
            gp.wait_ge(s.blk_done, 4)
            nc.gpsimd.memset(hrep[:, :, :], 0.0).then_inc(s.pads_set, 1)
            gp.wait_ge(s.vcmp_done, 1)
            nc.gpsimd.memset(pt[:, 4, :], 0.0).then_inc(s.pads_set, 1)
            nc.gpsimd.memset(spare[:, :], 0.0).then_inc(s.attn_done, 1)
            gp.wait_ge(s.attn_done, 2 * GQ + 1)
            gp.dma_start(pe_[:, :, :], ple_in).then_inc(s.ple_in, 16)
            squares(s.res_done, [4, 8, 12, 16], xt, 3, sqb, squ)
            squares(s.res_done, [4 * KT + n for n in (4, 8, 12, 16)], xt, 4, sqb, squ)
            squares(s.ple_done, [4, 8, 12, 16], xt, 5, sqb, squ)

        @block.scalar
        def _(act):
            def copy(dst, src):
                return nc.scalar.activation(dst, src, ACT.Copy)

            def split(g, i=0, per=RAW):
                if g >= LAST:
                    return
                n = g - WA0
                act.wait_ge(raw_ready[g % RAW], i * (2 * per) + 16 * (g // RAW + 1))
                act.wait_ge(quarters, i * (4 * per) + 4 * (n + 1))
                copy(whi[:, n % SPLIT, :], raw[:, g % RAW, :]).then_inc(hi_done, 1)

            def used(g):
                return 4 * (SPLIT + g - WA0) + 4

            def second_half(n, g7, i=0, per=RAW, bank=None):
                act.wait_ge(quarters, i * (4 * per) + 4 * (SPLIT + g7 - WA0) + n % 4 + 1)
                copy(half[:, n % 4, :], ps[n if bank is None else bank][:, T:2 * T]).then_inc(half_done, 1)

            def rms(use):
                act.wait_ge(s.ss_ps, use + 1)
                nc.scalar.activation(rs[:, :], ps[4][:, 0:T], ACT.Sqrt, bias=epsc[:, 0:1], scale=1.0 / D).then_inc(s.rms_done, 1)

            def scaled_hi(ready, first, src, gain, c):
                act.wait_ge(ready, first)
                nc.scalar.activation(acts[:, c, 0:T], src[:, c, :], ACT.Copy, scale=gain[:, c:c + 1]).then_inc(s.acts_hi, 1)

            act.wait_ge(s.eps_set, 2)
            act.wait_ge(s.loaded, 48)
            nc.scalar.activation(cact[:, :], vec[:, V_C:V_C + KT], ACT.Sigmoid).then_inc(s.cact_s, 1)
            for q in range(4):
                nc.scalar.activation(scr0[:, 4 * q:4 * q + 4, :], xt[:, 4 * q:4 * q + 4, :], ACT.Square).then_inc(s.sq_done, 1)
            rms(0)
            for g in range(WA0, WA0 + AHEAD):
                split(g)
            for c in range(KT):
                act.wait_ge(s.h_done, c + 1)
                copy(acts[:, c, 0:T], scr0[:, c, :]).then_inc(s.acts_hi, 1)
            with act.Fori(0, 8) as b:
                for j in range(8):
                    split(WA0 + j + AHEAD, b)
                for n in range(4):
                    second_half(n, WA0 + 7, b)
            for j in range(2):
                split(XW0 + j + AHEAD)
            second_half(3, XW0 + 1, bank=0)
            act.wait_ge(s.xz_mixed, 2)
            nc.scalar.activation(xz[0:HS, 0:T], t1[0:HS, :], ACT.Tanh).then_inc(s.xz_done, 1)
            copy(xz[HS:P, T:2 * T], t1[HS:P, :]).then_inc(s.xz_done, 1)

            with act.Fori(0, HT) as i:
                def weights(h):
                    if h % 2 == 0:
                        split(WB0 + h // 2 + AHEAD, i, 16)
                    if h % 16 == 15:
                        for n in range(4):
                            second_half(n, WB0 + h // 2, i, 16)
                    if h == 15:
                        act.wait_ge(evac_done, i * 8 + 37)
                        nc.scalar.activation(cz[:, :], stage[:, 3, :], ACT.Sigmoid).then_inc(s.zb_sig, 1)

                weights(0)
                act.wait_ge(s.vec_ready, i + 1)
                act.wait_ge(s.z_ps, i + 1)
                nc.scalar.activation(sw[:, :], ps[4][:, 0:T], ACT.Sigmoid, bias=hv[:, 3:4]).then_inc(s.gates_done, 1)
                nc.scalar.activation(aa[:, :], ps[4][:, T:2 * T], ACT.Sigmoid, bias=hv[:, 4:5]).then_inc(s.gates_done, 1)
                nc.scalar.activation(cz[:, :], tile_of(za, i), ACT.Sigmoid).then_inc(s.gates_done, 1)
                weights(1)
                weights(2)
                act.wait_ge(s.cum_ready, i + 1)
                nc.scalar.activation(each(pw), ca[:, :, 32:32 + CH], ACT.Exp).then_inc(s.exps_done, 1)
                nc.scalar.activation(each(pp), ca[:, :, 31:31 + CH], ACT.Exp).then_inc(s.exps_done, 1)
                nc.scalar.activation(each(pi), ca[:, :, 32:32 + CH], ACT.Exp, scale=-1.0).then_inc(s.exps_done, 1)
                act.wait_ge(s.kn_in, i + 1)
                nc.scalar.activation(t2[:, :], t2[:, :], ACT.Sqrt).then_inc(s.root_done, 1)
                weights(3)
                weights(4)
                act.wait_ge(s.mixed, i * 3 + 3)
                for n, (lo, hi) in enumerate(heads):
                    copy(vx[lo:hi, :, n * CH:(n + 1) * CH], each(vm)[lo:hi, :, :]).then_inc(s.vx_done, 1)
                for h in range(5, 10):
                    weights(h)
                act.wait_ge(s.m_ps, i + 1)
                copy(mi[:, :, :], four(6)).then_inc(s.m_first, 1)
                for n, (dst, bank) in enumerate(((ar, 7), (vx, 4))):
                    act.wait_ge(s.tr_ps, i * 4 + (n + 1))
                    copy(dst[:, :, 0:P], four(bank)).then_inc(s.tr_done, 1)
                weights(10)
                for n in range(1, 6):
                    act.wait_ge(s.t_ps, i * 5 + n)
                    copy(ts[:, :, :], four(6)).then_inc(s.t_done, 1)
                    if n in (1, 2):
                        act.wait_ge(s.tr_ps, i * 4 + (2 + n))
                        copy((bx, kx)[n - 1][:, :, :], four(5)).then_inc(s.tr_done, 1)
                    weights(9 + 2 * n)
                    weights(10 + 2 * n)
                act.wait_ge(s.w_ps, i + 1)
                copy(mi[:, :, :], four(6)).then_inc(s.w_done, 1)
                act.wait_ge(s.x_ps, i + 1)
                copy(ts[:, :, :], four(7)).then_inc(s.x_done, 1)
                weights(21)
                act.wait_ge(s.u2_ps, i + 1)
                copy(lt[:, :, :], four(5)).then_inc(s.u2_done, 1)
                for h in range(22, 31):
                    weights(h)
                act.wait_ge(s.var_ps, i + 1)
                nc.scalar.activation(t2[:, :], ps[5][:, T:2 * T], ACT.Sqrt, bias=epsc[:, 1:2]).then_inc(s.root_done, 1)
                weights(31)

            act.wait_ge(s.ya_done, HT)
            act.wait_ge(s.conv_done, HT)
            act.wait_ge(s.pool_moved, 64 * HT + 16)
            for n, buf in enumerate((k_, r_)):
                for c in range(HT):
                    copy(yab[:, n, c, 0:T], buf[:, c, 1:T + 1]).then_inc(s.yab_hi, 1)

            E = 33 + 8 * HT
            for b in range(4):
                g0 = PAB0 + 8 * b
                act.wait_ge(s.gab_in, 32 * (b + 1))
                for n in range(2):
                    nc.scalar.activation(gab[:, n, :, :], gab[:, n, :, :], ACT.Sigmoid).then_inc(s.gab_sig, 1)
                for j in range(8):
                    split(g0 + j + AHEAD)
                    if j == 3 or j == 7:
                        for n in range(4):
                            act.wait_ge(evac_done, E + 8 * b + j - 7 + n + 1)
                            second_half(n, g0 + j, bank=n + j // 4 * 4)
                for n in range(4):
                    act.wait_ge(s.m_sum, 4 * b + n + 1)
                    copy(acts[:, 4 * b + n, 0:T], m4[:, n, :]).then_inc(s.m_hi, 1)
            with act.Fori(0, 4) as b:
                for j in range(8):
                    split(WO0 + j + AHEAD, b)
                for n in range(4):
                    second_half(n, WO0 + 7, b)
            rms(1)
            E0 = E + 32 + KT + 4 * NG

            def first_block(g0, use, i=0):
                for j in range(8):
                    split(g0 + j + AHEAD, i)
                    if j == 5:
                        rms(use)
                for n in range(4):
                    second_half(n, g0 + 7, i)

            for c in range(KT):
                scaled_hi(s.x_done1, c // 4 + 1, xt, vec[:, V_MIX:V_MIX + KT], c)
            first_block(NS0, 2)
            with act.Fori(1, NG) as b:
                for j in range(8):
                    split(NS0 + j + AHEAD, b)
                for n in range(4):
                    second_half(n, NS0 + 7, b)
            split(GT0 + AHEAD)
            act.wait_ge(quarters, used(GT0))
            for q in range(2):
                act.wait_ge(s.rst_done, 1)
                nc.scalar.activation(gt[:, q, :], ps[4 + q][:, 0:GCOL], ACT.Sigmoid, scale=rst[:, q:q + 1]).then_inc(s.gt_done, 1)
            NB = GQ * NCMP
            for x in range(2):
                act.wait_ge(s.blk_f, 8 * x + 8)
                copy(blks[:, :, 0:NB], blkf[:, :, :]).then_inc(s.blk_hi, 1)
                for j in range(4):
                    split(CM0 + 4 * x + j + AHEAD)
                act.wait_ge(quarters, used(CM0 + 4 * x + 3))
                copy(hid[:, 2, :], ps[6 + x][:, NB:2 * NB]).then_inc(s.hid_half, 1)
                act.wait_ge(s.hid_sum, x + 1)
                nc.scalar.activation(hid[:, 2, :], hid[:, x, :], ACT.Sigmoid).then_inc(s.hid_sig, 1)
            act.wait_ge(s.vcmp_done, 1)
            act.wait_ge(s.scaled, 4 * NG)
            with act.Fori(0, GQ) as g:
                copy(ng[:, 4:8, :], nsb[:, bass.ds(g * NG + 4, 4), :]).then_inc(s.ng_done, 1)
                act.wait_ge(s.v_ps, g + 1)
                copy(vtm[:, :, :], four(7)).then_inc(s.vtm_done, 1)
                for q in (1, 0):
                    act.wait_ge(s.max_done, g * 2 + (2 - q))
                    for j in range(HPG):
                        for x in range(2):
                            K = (q + 1) * P
                            src = ps[j][:, x * T:x * T + T] if q else ps[5 + j // 2][:, (j % 2 * 2 + x) * P:(j % 2 * 2 + x + 1) * P]
                            dst = (pr1 if q else pr0)[:, j, x * K:(x + 1) * K]
                            nc.scalar.activation(dst, src, ACT.Exp, bias=nm[:, x, q * HPG + j:q * HPG + j + 1], scale=DH ** -0.5,
                                                 accum_out=su[:, x, q * HPG + j:q * HPG + j + 1]).then_inc(s.exp_done, 1)
                    if q:
                        act.wait_ge(s.cd_done, g + 1)
                        nc.scalar.activation(pc[:, :, :], pc[:, :, :], ACT.Exp, scale=DH ** -0.5).then_inc(s.cexp_done, 1)
                for q in (1, 0):
                    for n in range(4 if q else 2):
                        act.wait_ge(s.p_ps, g * 8 + ((n + 1) if q else (6 + n)))
                        if n % 2 == 0:
                            copy(pt[:, n, :], ps[n if q else 5 + n][:, :]).then_inc(s.pt_act, 1)
                    act.wait_ge(s.p_ps, g * 8 + (5 if q else 8))
                    act.wait_ge(s.pads_set, 3)
                    for j in range(HPG):
                        lo = NP32 * j
                        copy(pt[lo:lo + NP32, 4, j * P:(j + 1) * P], ps[4][lo:lo + NP32, (1 - q) * P:(2 - q) * P]
                             ).then_inc(s.pt_act, 1)
                    act.wait_ge(s.o_ps, g * 2 + (2 - q))
                    copy(acts[:, bass.ds(g * HPG, HPG), q * P:(q + 1) * P], four(7 if q else 4)).then_inc(s.o_hi, 1)
            with act.Fori(0, 4) as b:
                for j in range(8):
                    split(NO0 + j + AHEAD, b)
                for n in range(4):
                    second_half(n, NO0 + 7, b)
            act.wait_ge(quarters, used(NO0 + 31))
            for c in range(KT):
                scaled_hi(s.res_done, c + 1, xt, vec[:, V_FFN:V_FFN + KT], c)
            act.wait_ge(s.ple_in, 16)
            copy(pes[:, :, 0:T], pe_[:, :, :]).then_inc(s.pes_hi, 1)

            def relu_hi(i, b):
                for n in range(4):
                    act.wait_ge(s.relu_done, i + (n + 1))
                    copy(tile_of(hff, b * 4 + n, 0, T), q4[:, n, :]).then_inc(s.relu_hi, 1)

            def ffn(f, first):
                if first:
                    first_block(FF0, 3)
                    relu_hi(0, 0)
                with act.Fori(1 if first else 0, 4) as b:
                    for j in range(8):
                        split(FF0 + j + AHEAD, f * 8 + b)
                    for n in range(4):
                        second_half(n, FF0 + 7, f * 8 + b)
                    relu_hi(f * 16 + b * 4, b)
                with act.Fori(0, 4) as b:
                    for j in range(8):
                        split(FF0 + 32 + j + AHEAD, f * 8 + b)
                    for n in range(4):
                        second_half(n, FF0 + 32 + 7, f * 8 + b)

            ffn(0, True)
            with act.Fori(1, 4) as f:
                ffn(f, False)
            for b in range(4):
                split(PR0 + b + AHEAD)
                for n in range(4):
                    act.wait_ge(evac_done, E0 + 9 * KT + 4 * b - 4 + n + 1)
                    second_half(n, PR0 + b)
                for c in range(4 * b, 4 * b + 4):
                    scaled_hi(s.res_done, 4 * KT + c + 1, xt, vec[:, V_PLE:V_PLE + KT], c)

            def ple_gate(b, last, first=False):
                for j in range(8):
                    if not (last and j + AHEAD >= 8):
                        split(PG0 + j + AHEAD, b)
                    if first and j == 5:
                        rms(4)
                for n in range(4):
                    second_half(n, PG0 + 7, b)
                for n in range(4):
                    act.wait_ge(s.scaled, b * 4 + (4 * NG + n + 1))
                    nc.scalar.activation(q4[:, n, :], s4[:, n, :], ACT.Sigmoid).then_inc(s.pg_sig, 1)

            ple_gate(0, False, True)
            with act.Fori(1, 3) as b:
                ple_gate(b, False)
            ple_gate(3, True)
            rms(5)

        @block.vector
        def _(dve):
            V = Steps(dve, s.dve_step)
            tt, ts2, stt = nc.vector.tensor_tensor, nc.vector.tensor_scalar, nc.vector.scalar_tensor_tensor

            def split(g, i=0, per=RAW):
                if g >= LAST:
                    return
                n = g - WA0
                dve.wait_ge(hi_done, i * per + (n + 1))
                tt(wlo[:, n % SPLIT, :], raw[:, g % RAW, :], whi[:, n % SPLIT, :].bitcast(F32), ALU.subtract
                   ).then_inc(raw_used, 1)

            def first_half(dst, n, e, i=0, bank=None):
                dve.wait_ge(half_done, i + (e + 1))
                return tt(dst, ps[n if bank is None else bank][:, 0:T], half[:, n % 4, :], ALU.add).then_inc(evac_done, 1)

            def scaled_lo(k, src, gain, c):
                dve.wait_ge(s.acts_hi, KT * k + c + 1)
                stt(acts[:, c, T:2 * T], src[:, c, :], gain[:, c:c + 1], acts[:, c, 0:T].bitcast(F32), ALU.mult, ALU.subtract
                    ).then_inc(s.acts_ready, 1)

            def rs_of(use):
                dve.wait_ge(s.rms_done, use + 1)
                nc.vector.reciprocal(rs[:, :], rs[:, :]).then_inc(s.rs_ready, 1)
                dve.wait_ge(s.rs_ready, use - 1)

            dve.wait_ge(s.cact_s, 1)
            V.step(tt(cact[:, :], cact[:, :], vec[:, V_C:V_C + KT], ALU.mult))

            def ada_block(b):
                for j in range(KT):
                    dve.wait_ge(raw_ready[j % RAW], b * 32 + 16 * (j // RAW + 1))
                    dst = acc[:, bass.ds(b * CW, CW)]
                    if j == 0:
                        ts2(dst, raw[:, 0, :], cact[:, 0:1], None, ALU.mult).then_inc(raw_used, 1)
                    else:
                        dve.wait_ge(raw_used, b * KT + (RAW + j))
                        stt(dst, raw[:, j % RAW, :], cact[:, j:j + 1], dst, ALU.mult, ALU.add).then_inc(raw_used, 1)

            ada_block(0)
            dve.wait_ge(s.rms_done, 1)
            V.step(nc.vector.reciprocal(rs[:, :], rs[:, :]))
            for c in range(KT):
                V.do(tt(scr0[:, c, :], xt[:, c, :], rs[:, :], ALU.mult))
            with dve.Fori(1, 2 * D // CW) as b:
                ada_block(b)
            for g in range(WA0, WA0 + AHEAD):
                split(g)
            dve.wait_ge(s.mod_ps, 1)
            V.step(tt(mod[:, 0:2 * KT], ps[5][:, 0:2 * KT], vec[:, V_ADAB:V_ADAB + 2 * KT], ALU.add))
            V.step(ts2(gpre[:, :], mod[:, KT:2 * KT], 1.0, None, ALU.add))
            V.step(tt(gpre[:, :], gpre[:, :], vec[:, V_PRE:V_PRE + KT], ALU.mult))
            for c in range(KT + 2):
                if c < KT:
                    ts2(scr0[:, c, :], scr0[:, c, :], gpre[:, c:c + 1], mod[:, c:c + 1], ALU.mult, ALU.add).then_inc(s.h_done, 1)
                if c >= 2:
                    dve.wait_ge(s.acts_hi, c - 1)
                    tt(acts[:, c - 2, T:2 * T], scr0[:, c - 2, :], acts[:, c - 2, 0:T].bitcast(F32), ALU.subtract
                       ).then_inc(s.acts_ready, 1)

            dve.wait_ge(s.init_done, 10)
            for x, buf in enumerate((r_, k_, v_, za)):
                with dve.Fori(0, 2) as b:
                    dve.wait_ge(s.gate_used, b * 4 + (8 * x + 4))
                    nc.vector.tensor_copy(cg[:, :], cact[:, bass.ds(b * 4 + x % 2 * 8, 4)]).then_inc(s.cg_done, 1)
                    for j in range(8):
                        split(WA0 + 16 * x + j + AHEAD, b)
                        if j % 2:
                            m = j // 2
                            dst = gacc[:, x // 2 * CW:x // 2 * CW + CW]
                            dve.wait_ge(s.cg_done, b + (2 * x + 1))
                            dve.wait_ge(gate_in[m], b * 16 + 16 * (2 * x + 1))
                            dve.wait_ge(s.gate_used, b * 4 + (8 * x + m + 4))
                            stt(dst, graw[:, m, :], cg[:, m:m + 1], dst, ALU.mult, ALU.add).then_inc(s.gate_used, 1)
                    for n in range(4):
                        lo = 0 if buf is za else 1
                        first_half(one(buf[:, bass.ds(b * 4 + n, 1), lo:lo + T]), n, 8 * x + n, b * 4)
            for j in range(2):
                split(XW0 + j + AHEAD)
            first_half(cu[:, 2:T + 2], 3, 32, bank=0)
            dve.wait_ge(evac_done, 33)
            V.step(tt(t1[:, :], cu[:, 1:T + 1], cu[:, 2:T + 2], ALU.subtract))
            stt(t1[0:HS, :], t1[0:HS, :], vec[0:HS, V_MUX:V_MUX + 1], cu[0:HS, 2:T + 2], ALU.mult, ALU.add).then_inc(s.xz_mixed, 1)
            stt(t1[HS:P, :], t1[HS:P, :], vec[HS:P, V_MUX:V_MUX + 1], cu[HS:P, 2:T + 2], ALU.mult, ALU.add).then_inc(s.xz_mixed, 1)
            dve.wait_ge(s.xz_done, 2)

            dve.wait_ge(s.gate_ps, 1)
            V.step(tt(mod[:, 2 * KT:3 * KT], ps[5][:, 0:KT], vec[:, V_ADAB + 2 * KT:V_ADAB + 3 * KT], ALU.add))
            V.do(tt(gpost[:, :], mod[:, 2 * KT:3 * KT], vec[:, V_POST:V_POST + KT], ALU.mult))
            dve.wait_ge(s.ar_zero, 1)
            dve.wait_ge(s.pool_moved, 16)

            with dve.Fori(0, HT) as i:
                V.enter(i, DVE_STEPS)

                def weights(h):
                    if h % 2 == 0:
                        split(WB0 + h // 2 + AHEAD, i, 16)
                    if h == 15:
                        for n in range(4):
                            dve.wait_ge(half_done, i * 8 + (34 + n))
                            tt(stage[:, n, :], ps[n][:, 0:T], half[:, n, :], ALU.add).then_inc(evac_done, 1)
                        dve.wait_ge(evac_done, i * 8 + 37)
                        V.do(tt(stage[:, 2, :], stage[:, 2, :], stage[:, 3, :], ALU.mult))
                        V.step(tt(cu[:, 2:T + 2], stage[:, 0, :], stage[:, 1, :], ALU.mult))
                        V.step(ts2(cy[:, :], cu[:, 2:T + 2], hc[:, 2:3], None, ALU.mult))
                        V.step(stt(cy[:, :], cu[:, 1:T + 1], hc[:, 1:2], cy[:, :], ALU.mult, ALU.add))
                        V.step(stt(cy[:, :], cu[:, 0:T], hc[:, 0:1], cy[:, :], ALU.mult, ALU.add))
                        V.step(tt(cy[:, :], cy[:, :], stage[:, 2, :], ALU.mult))
                        dve.wait_ge(s.zb_sig, i + 1)
                        tt(tile_of(k_, i, 1, T + 1), cy[:, :], cz[:, :], ALU.mult).then_inc(s.conv_done, 1)
                    if h == 31:
                        dve.wait_ge(s.pool_moved, i * 64 + 16)
                        for n in range(4):
                            dve.wait_ge(half_done, i * 8 + (38 + n))
                            tt(stage[:, 4 + n, :], ps[n][:, 0:T], half[:, n, :], ALU.add).then_inc(evac_done, 1)

                nc.vector.tensor_copy(hv[:, :], vec[:, bass.ds(i * HPV, HPV)]).then_inc(s.vec_ready, 1)
                nc.vector.tensor_copy(lw[:, :], lora[:, bass.ds(i * P, P)]).then_inc(s.lora_ready, 1)
                V.do(nc.vector.tensor_copy(hc[:, :], vec[:, bass.ds(i * 3 + V_CONV, 3)]))
                for x, buf in enumerate((r_, k_, v_)):
                    V.do(tt((rm, km, vm)[x][:, :], tile_of(buf, i, 0, T), tile_of(buf, i, 1, T + 1), ALU.subtract))
                V.wait()
                dve.wait_ge(s.vec_ready, i + 1)
                for x, buf in enumerate((r_, k_, v_)):
                    t = (rm, km, vm)[x][:, :]
                    stt(t, t, hv[:, x:x + 1], tile_of(buf, i, 1, T + 1), ALU.mult, ALU.add).then_inc(s.mixed, 1)
                weights(0)
                dve.wait_ge(s.mixed, i * 3 + 3)
                V.do(ts2(kk[:, :], km[:, :], hv[:, 5:6], None, ALU.mult))
                V.step(ts2(rm2[:, :], rm[:, :], hv[:, 7:8], None, ALU.mult))
                tt(t2[:, :], kk[:, :], kk[:, :], ALU.mult).then_inc(s.sq_ready, 1)
                weights(1)
                dve.wait_ge(s.gates_done, i * 3 + 1)
                V.step(ts2(ca[:, :, 32:32 + CH], each(sw), -EXP_M_HALF, None, ALU.mult))
                src, dst = ca, cb
                for n in range(6):
                    ins = tt(dst[:, :, 32:32 + CH], src[:, :, 32:32 + CH], src[:, :, 32 - 2 ** n:32 + CH - 2 ** n], ALU.add)
                    if n == 5:
                        ins.then_inc(s.cum_ready, 1)
                    else:
                        V.step(ins)
                    src, dst = dst, src
                weights(2)
                dve.wait_ge(s.gates_done, i * 3 + 3)
                V.do(ts2(t1[:, :], aa[:, :], -1.0, hv[:, 6:7], ALU.add, ALU.mult))
                V.wait()
                dve.wait_ge(s.ss2_ps, i + 1)
                ts2(t2[:, :], ps[5][:, 0:T], 1e-24, None, ALU.max).then_inc(s.kn_in, 1)
                V.step(stt(kp[:, :], t1[:, :], 1.0, km[:, :], ALU.add, ALU.mult))
                tt(t1[:, :], rm2[:, :], kp[:, :], ALU.mult).then_inc(s.br_ready, 1)
                dve.wait_ge(s.root_done, i * 2 + 1)
                V.step(nc.vector.reciprocal(t2[:, :], t2[:, :]))
                V.step(tt(kk[:, :], kk[:, :], t2[:, :], ALU.mult))
                V.step(tt(rm2[:, :], kk[:, :], aa[:, :], ALU.mult))
                weights(3)
                weights(4)
                dve.wait_ge(s.exps_done, i * 3 + 3)
                for n, (lo, hi) in enumerate(heads):
                    c0 = n * CH
                    part = lambda t: each(t)[lo:hi, :, :]
                    stt(ar[lo:hi, :, c0:c0 + CH], part(pp), -1.0, part(kk), ALU.mult, ALU.mult).then_inc(s.ops_done, 1)
                    tt(ar[lo:hi, :, P + c0:P + c0 + CH], part(pw), part(rm), ALU.mult).then_inc(s.ops_done, 1)
                    tt(bx[lo:hi, :, c0:c0 + CH], part(rm2), part(pi), ALU.mult).then_inc(s.ops_done, 1)
                    tt(kx[lo:hi, :, c0:c0 + CH], part(kp), part(pi), ALU.mult).then_inc(s.ops_done, 1)
                dve.wait_ge(s.bs_ps, i + 1)
                tt(aa[:, :], ps[5][:, T:2 * T], vm[:, :], ALU.mult).then_inc(s.bon_done, 1)
                V.do(tt(tile_of(za, i), tile_of(za, i), cz[:, :], ALU.mult))
                weights(5)
                weights(6)

                def mask(c, bank):
                    dve.wait_ge(s.g_ps, i * 4 + (c + 1))
                    tt(gm[:, c, :], ps[bank][:, :], con[:, C_G:C_G + 4 * P], ALU.mult).then_inc(s.gm_done, 1)

                mask(0, 6)
                mask(1, 7)
                weights(7)
                mask(2, 4)
                mask(3, 5)
                dve.wait_ge(s.gm_done, i * 4 + 4)
                V.step(tt(mt[:, :, :], gm[:, :, 0:P], tri(0), ALU.mult))
                tt(mt[:, :, :], mt[:, :, :], ident4, ALU.add).then_inc(s.mt_upd, 1)
                tt(lt[:, :, :], gm[:, :, 0:P], tri(1), ALU.mult).then_inc(s.lt_ready, 1)
                for t in (bx, kx):
                    tt(t[:, :, :], t[:, :, :], each(pw)[:, :, CH - 1:CH].to_broadcast([P, NC, P]), ALU.mult
                       ).then_inc(s.bk_scaled, 1)
                for h in range(8, 11):
                    weights(h)
                for n in range(1, 6):
                    weights(9 + 2 * n)
                    if n == 1:
                        dve.wait_ge(s.m_first, i + 1)
                    if n < 5:
                        dve.wait_ge(s.u_ps, i * 4 + n)
                        tt(mi[:, :, :], mi[:, :, :], four(7), ALU.add).then_inc(s.m_upd, 1)
                    dve.wait_ge(s.ut_ps, i * 5 + n)
                    tt(mt[:, :, :], mt[:, :, :], four(4), ALU.add).then_inc(s.mt_upd, 1)
                    if n < 5:
                        tt(lt[:, :, :], gm[:, :, 0:P], tri(n + 1), ALU.mult).then_inc(s.lt_ready, 1)
                    weights(10 + 2 * n)
                weights(21)
                weights(22)
                decay = lambda c: pw[:, c * CH + CH - 1:c * CH + CH]
                dve.wait_ge(s.d_ps, i * 3 + 1)
                nc.vector.tensor_copy(st[:, 0, :], ps[7][:, 0:P]).then_inc(s.s_done, 1)
                weights(23)
                for c in range(1, NC):
                    dve.wait_ge(s.sa_ps, i * 3 + c)
                    tt(sa[:, c % 2, :], ps[6][:, 0:P], lt[:, c, :], ALU.add).then_inc(s.sa_done, 1)
                    weights(22 + 2 * c)
                    if c < NC - 1:
                        dve.wait_ge(s.d_ps, i * 3 + (c + 1))
                        dve.wait_ge(s.s_done, i * 3 + c)
                        stt(st[:, c % 2, :], st[:, 1 - c % 2, :], decay(c), ps[7][:, 0:P], ALU.mult, ALU.add
                            ).then_inc(s.s_done, 1)
                        weights(23 + 2 * c)
                dve.wait_ge(s.y_ps, i + 1)
                for n, (lo, hi) in enumerate(heads):
                    nc.vector.tensor_copy(each(t1)[lo:hi, :, :], four(4)[lo:hi, :, n * CH:(n + 1) * CH]).then_inc(s.yc_done, 1)
                weights(29)
                dve.wait_ge(s.mu_ps, i + 1)
                V.step(tt(t1[:, :], t1[:, :], ps[5][:, 0:T], ALU.subtract))
                tt(t2[:, :], t1[:, :], t1[:, :], ALU.mult).then_inc(s.ysq_done, 1)
                V.do(ts2(t1[:, :], t1[:, :], hv[:, 8:9], None, ALU.mult))
                weights(30)
                dve.wait_ge(s.root_done, i * 2 + 2)
                V.step(nc.vector.reciprocal(t2[:, :], t2[:, :]))
                V.step(tt(t1[:, :], t1[:, :], t2[:, :], ALU.mult))
                V.step(stt(t1[:, :], t1[:, :], hv[:, 9:10], aa[:, :], ALU.add, ALU.add))
                tt(tile_of(r_, i, 1, T + 1), t1[:, :], tile_of(za, i), ALU.mult).then_inc(s.ya_done, 1)
                weights(31)
            V.leave(HT)

            for n, buf in enumerate((k_, r_)):
                for c in range(HT):
                    dve.wait_ge(s.yab_hi, HT * n + c + 1)
                    tt(yab[:, n, c, T:2 * T], buf[:, c, 1:T + 1], yab[:, n, c, 0:T].bitcast(F32), ALU.subtract
                       ).then_inc(s.yab_done, 1)
            E = 33 + 8 * HT
            for b in range(4):
                g0 = PAB0 + 8 * b
                for j in range(8):
                    split(g0 + j + AHEAD)
                    if j == 3 or j == 7:
                        x = j // 4
                        dve.wait_ge(s.gab_sig, 2 * b + x + 1)
                        for n in range(4):
                            e = E + 8 * b + 4 * x + n
                            dst = (m4, m5)[x][:, n, :]
                            first_half(dst, n, e, bank=n + 4 * x)
                            dve.wait_ge(evac_done, e + 1)
                            tt(dst, dst, gab[:, x, n, :], ALU.mult).then_inc(s.mul_done, 1)
                for n in range(4):
                    dve.wait_ge(s.mul_done, 8 * b + 4 + n + 1)
                    tt(m4[:, n, :], m4[:, n, :], m5[:, n, :], ALU.add).then_inc(s.m_sum, 1)
                for n in range(4):
                    dve.wait_ge(s.m_hi, 4 * b + n + 1)
                    tt(acts[:, 4 * b + n, T:2 * T], m4[:, n, :], acts[:, 4 * b + n, 0:T].bitcast(F32), ALU.subtract
                       ).then_inc(s.m_done, 1)
            E += 32
            with dve.Fori(0, 4) as b:
                for j in range(8):
                    split(WO0 + j + AHEAD, b)
                for n in range(4):
                    first_half(tile_of(ob, b * 4 + n), n, E + n, b * 4)
            E += 16
            dve.wait_ge(evac_done, E)
            dve.wait_ge(s.rms_done, 2)
            V.step(nc.vector.reciprocal(rs[:, :], rs[:, :]))
            dve.wait_ge(s.x_again, 16)
            gain = vec[:, V_MIX:V_MIX + KT]
            for q in range(5):
                if q < 4:
                    for c in range(4 * q, 4 * q + 4):
                        V.do(stt(ob[:, c, :], ob[:, c, :], gpost[:, c:c + 1], rs[:, :], ALU.mult, ALU.mult))
                    V.wait()
                    tt(xt[:, 4 * q:4 * q + 4, :], xt[:, 4 * q:4 * q + 4, :], ob[:, 4 * q:4 * q + 4, :], ALU.add
                       ).then_inc(s.x_done1, 1)
                if q:
                    for c in range(4 * q - 4, 4 * q):
                        scaled_lo(1, xt, gain, c)
            def scaled_block(g0, e, dst, b, first=None, drop=0):
                for j in range(8):
                    if j + AHEAD < 8 or not drop:
                        split(g0 + j + AHEAD, b)
                    if j == 6 and first is not None:
                        rs_of(first)
                for n in range(4):
                    first_half(dst(n), n, e + n, b * 4)
                for n in range(4):
                    dve.wait_ge(evac_done, b * 4 + (e + n + 1))
                    tt(dst(n), dst(n), rs[:, :], ALU.mult).then_inc(s.scaled, 1)

            scaled_block(NS0, E, lambda n: nsb[:, n, :], 0, first=2)
            with dve.Fori(1, NG) as b:
                scaled_block(NS0, E, lambda n: tile_of(nsb, b * 4 + n), b)
            E += 4 * NG
            dve.wait_ge(s.rst_ps, 1)
            for q in range(2):
                ins = nc.vector.tensor_copy(rst[:, q:q + 1], ps[6][:, q * P:q * P + 1])
            ins.then_inc(s.rst_done, 1)
            split(GT0 + AHEAD)
            dve.wait_ge(s.scaled, 4 * NG)
            NB = GQ * NCMP
            for x in range(2):
                for g in range(GQ):
                    kv = nsb[:, g * NG + G_KC + x, :]
                    first = kv.rearrange("p (n l) -> p l n", l=CS)
                    for h in range(2):
                        pos = vec[:, (V_POSK, V_POSV)[x] + h * CS:(V_POSK, V_POSV)[x] + (h + 1) * CS]
                        tt(blkf[:, h * CS:(h + 1) * CS, g * NCMP:(g + 1) * NCMP], first[:, :, h:h + NCMP],
                                pos.rearrange("p (l n) -> p l n", n=1).to_broadcast([P, CS, NCMP]), ALU.add).then_inc(s.blk_f, 1)
                dve.wait_ge(s.blk_f, 8 * x + 8)
                dve.wait_ge(s.blk_hi, x + 1)
                tt(blks[:, :, NB:2 * NB], blkf[:, :, :], blks[:, :, 0:NB].bitcast(F32), ALU.subtract).then_inc(s.blk_lo, 1)
                for j in range(4):
                    split(CM0 + 4 * x + j + AHEAD)
                dve.wait_ge(s.hid_half, x + 1)
                tt(hid[:, x, :], ps[6 + x][:, 0:NB], hid[:, 2, :], ALU.add).then_inc(s.hid_sum, 1)
                dve.wait_ge(s.hid_sig, x + 1)
                if x == 0:
                    tt(hid[:, 0, :], hid[:, 0, :], hid[:, 2, :], ALU.mult).then_inc(s.blk_done, 1)
                else:
                    tt(hid[:, 1, :], hid[:, 1, :], hid[:, 2, :], ALU.mult).then_inc(s.blk_done, 3)
                    dve.wait_ge(s.blk_done, 4)
                    dve.wait_ge(s.pads_set, 2)
                    for g in range(GQ):
                        nc.vector.tensor_copy(
                            hrep[:, g, :].rearrange("p (h n) -> p h n", h=HPG)[:, :, 0:NCMP],
                            hid[:, 1:2, g * NCMP:(g + 1) * NCMP].to_broadcast([P, HPG, NCMP])).then_inc(s.hrep_done, 1)
            dve.wait_ge(s.cmp_ps, 1)
            nc.vector.tensor_copy(kcmp[:, :, 0:NCMP], ps[4][:, 0:NB].rearrange("p (g n) -> p g n", g=GQ)).then_inc(s.kcmp_done, 1)
            dve.wait_ge(s.cmp_ps, 2)
            nc.vector.tensor_copy(vcmp[:, :, :], four(5)).then_inc(s.vcmp_done, 1)
            caus4 = con[:, C_CAU:C_CAU + P].rearrange("p (a n) -> p a n", a=1).to_broadcast([P, 4, P])
            dve.wait_ge(s.kcmp_done, 1)
            dve.wait_ge(s.gt_done, 2)
            with dve.Fori(0, GQ) as g:
                V.enter(g, ATTN_STEPS)
                dve.wait_ge(s.vcmp_done, 1)
                nc.vector.tensor_copy(kcg[:, :], one(kcmp[:, bass.ds(g, 1), :])).then_inc(s.ng_dve, 1)
                nc.vector.tensor_copy(vcg[:, :], one(vcmp[:, bass.ds(g, 1), :])).then_inc(s.ng_dve, 1)
                V.do(nc.vector.tensor_copy(gg[:, :, :], gt[:, :, bass.ds(g * 3 * HPG, 3 * HPG)]))
                nc.vector.tensor_copy(ng[:, 0:4, :], nsb[:, bass.ds(g * NG, 4), :]).then_inc(s.ng_dve, 1)
                for q in (1, 0):
                    dve.wait_ge(s.s_ps, g * 3 + (1 if q else 2))
                    banks = range(4) if q else (5, 6)
                    for n, bank in enumerate(banks):
                        v = ps[bank][:, :].rearrange("p (x k) -> p x k", k=(q + 1) * P)[:, :, q * P:(q + 1) * P]
                        V.do(tt(v, v, con[:, C_CAU:C_CAU + P].rearrange("p (a n) -> p a n", a=1).to_broadcast(
                            [P, 4 - 2 * q, P]), ALU.add))
                    V.wait()
                    for n, bank in enumerate(banks):
                        if q:
                            V.do(nc.vector.tensor_reduce(mx[:, 0:2, HPG + n], ps[bank][:, :].rearrange("p (x k) -> p x k", x=2),
                                                         AX_X, ALU.max))
                        else:
                            V.do(nc.vector.tensor_reduce(
                                mx[:, 0:2, 2 * n:2 * n + 2].rearrange("p x h -> p h x"),
                                ps[bank][:, :].rearrange("p (h x k) -> p h x k", h=2, x=2), AX_X, ALU.max))
                    V.wait()
                    c = slice(HPG, 2 * HPG) if q else slice(0, HPG)
                    ts2(nm[:, :, c], mx[:, 0:2, c], -DH ** -0.5, None, ALU.mult).then_inc(s.max_done, 1)
                    if q:
                        dve.wait_ge(s.s_ps, g * 3 + 3)
                        for t in range(2):
                            v = ps[4][:, t * P:(t + 1) * P].rearrange("p (h n) -> p h n", h=HPG)
                            w = con[:, C_NEG + (1 - t) * NP32:C_NEG + (2 - t) * NP32].rearrange("p (a n) -> p a n", a=1)
                            V.do(tt(v, v, w.to_broadcast([P, HPG, NP32]), ALU.add))
                        V.wait()
                        pcv = ps[4][:, 0:2 * P].rearrange("p (h n) -> p h n", n=NP32)
                        V.step(nc.vector.tensor_reduce(mx[:, 2, :], pcv, AX_X, ALU.max))
                        tt(pc[:, :, :], pcv, mx[:, 2, :].rearrange("p (h n) -> p h n", n=1).to_broadcast([P, 2 * HPG, NP32]),
                           ALU.subtract).then_inc(s.cd_done, 1)
                dve.wait_ge(s.cexp_done, g + 1)
                V.step(nc.vector.tensor_reduce(su[:, 2, :], pc[:, :, :], AX_X, ALU.add))
                for t in range(2):
                    w = con[:, C_VAL + (1 - t) * NP32:C_VAL + (2 - t) * NP32].rearrange("p (a n) -> p a n", a=1)
                    v = pc[:, t * HPG:(t + 1) * HPG, :]
                    V.do(tt(v, v, w.to_broadcast([P, HPG, NP32]), ALU.mult))
                dve.wait_ge(s.exp_done, g * 16 + 16)
                V.step(nc.vector.reciprocal(su[:, :, :], su[:, :, :]))
                for x, branch in enumerate((1, 2, 0)):
                    for q in range(2):
                        t = q if x < 2 else 1 - q
                        v = su[:, x, t * HPG:(t + 1) * HPG]
                        V.do(tt(v, v, gg[:, q, :].rearrange("p (h b) -> p b h", b=3)[:, branch, :], ALU.mult))
                V.wait()
                for q in (1, 0):
                    K = (q + 1) * P
                    for j in range(HPG):
                        for x in range(2):
                            v = (pr1 if q else pr0)[:, j, x * K:(x + 1) * K]
                            ts2(v, v, su[:, x, q * HPG + j:q * HPG + j + 1], None, ALU.mult).then_inc(s.pr_done, 1)
                    v = pc[:, (1 - q) * HPG:(2 - q) * HPG, :]
                    tt(v, v, su[:, 2, (1 - q) * HPG:(2 - q) * HPG].rearrange("p (h n) -> p h n", n=1).to_broadcast([P, HPG, NP32]),
                       ALU.mult).then_inc(s.pr_done, 1)
                for q in (1, 0):
                    for n in range(4 if q else 2):
                        if n % 2:
                            dve.wait_ge(s.p_ps, g * 8 + ((n + 1) if q else (6 + n)))
                            nc.vector.tensor_copy(pt[:, n, :], ps[n if q else 5 + n][:, :]).then_inc(s.pt_dve, 1)
                    dve.wait_ge(s.o_hi, g * 2 + (2 - q))
                    tt(acts[:, bass.ds(g * HPG, HPG), T + q * P:T + (q + 1) * P], four(7 if q else 4),
                       acts[:, bass.ds(g * HPG, HPG), q * P:(q + 1) * P].bitcast(F32), ALU.subtract).then_inc(s.attn_done, 1)
            V.leave(GQ)

            with dve.Fori(0, 4) as b:
                for j in range(8):
                    split(NO0 + j + AHEAD, b)
                for n in range(4):
                    first_half(s4[:, n, :], n, E + n, b * 4)
                for n in range(4):
                    dve.wait_ge(evac_done, b * 4 + (E + n + 1))
                    v = tile_of(xt, b * 4 + n)
                    tt(v, v, s4[:, n, :], ALU.add).then_inc(s.res_done, 1)
            E += KT
            for c in range(KT):
                scaled_lo(2, xt, vec[:, V_FFN:V_FFN + KT], c)
            dve.wait_ge(s.pes_hi, 1)
            tt(pes[:, :, T:2 * T], pe_[:, :, :], pes[:, :, 0:T].bitcast(F32), ALU.subtract).then_inc(s.pes_lo, 1)

            def relu_block(f, b, i, first):
                for j in range(8):
                    split(FF0 + j + AHEAD, i)
                    if first and j == 6:
                        rs_of(3)
                for n in range(4):
                    first_half(s4[:, n, :], n, E + n, i * 4)
                for n in range(4):
                    dve.wait_ge(evac_done, i * 4 + (E + n + 1))
                    stt(s4[:, n, :], s4[:, n, :], 0.0, rs[:, :], ALU.max, ALU.mult).then_inc(s.relu_rs, 1)
                for n in range(4):
                    dve.wait_ge(s.relu_rs, f * 16 + b * 4 + (n + 1))
                    tt(q4[:, n, :], s4[:, n, :], s4[:, n, :], ALU.mult).then_inc(s.relu_done, 1)
                for n in range(4):
                    dve.wait_ge(s.relu_hi, f * 16 + b * 4 + (n + 1))
                    tt(tile_of(hff, b * 4 + n, T, 2 * T), q4[:, n, :], tile_of(hff, b * 4 + n, 0, T).bitcast(F32),
                       ALU.subtract).then_inc(s.relu_lo, 1)

            def ffn(f, first):
                if first:
                    relu_block(0, 0, 0, True)
                with dve.Fori(1 if first else 0, 4) as b:
                    relu_block(f, b, f * 8 + b, False)
                with dve.Fori(0, 4) as b:
                    i = f * 8 + b
                    for j in range(8):
                        split(FF0 + 32 + j + AHEAD, i)
                    for n in range(4):
                        first_half(s4[:, n, :], n, E + 16 + n, i * 4)
                    for n in range(4):
                        dve.wait_ge(evac_done, i * 4 + (E + 16 + n + 1))
                        v = tile_of(xt, b * 4 + n)
                        tt(v, v, s4[:, n, :], ALU.add).then_inc(s.res_done, 1)

            ffn(0, True)
            with dve.Fori(1, 4) as f:
                ffn(f, False)
            E += 128
            for b in range(4):
                split(PR0 + b + AHEAD)
                for n in range(4):
                    first_half(pj[:, 4 * b + n, :], n, E + 4 * b + n)
                for c in range(4 * b, 4 * b + 4):
                    scaled_lo(3, xt, vec[:, V_PLE:V_PLE + KT], c)
            E += KT

            def ple_gate(b, last, first=None):
                scaled_block(PG0, E, lambda n: s4[:, n, :], b, first, drop=last)
                for n in range(4):
                    dve.wait_ge(s.pg_sig, b * 4 + (n + 1))
                    tt(q4[:, n, :], q4[:, n, :], tile_of(pj, b * 4 + n), ALU.mult).then_inc(s.pg_mul, 1)
                for n in range(4):
                    dve.wait_ge(s.pg_mul, b * 4 + (n + 1))
                    v = tile_of(xt, b * 4 + n)
                    tt(v, v, q4[:, n, :], ALU.add).then_inc(s.ple_done, 1)

            ple_gate(0, False, 4)
            with dve.Fori(1, 3) as b:
                ple_gate(b, False)
            ple_gate(3, True)
            dve.wait_ge(s.rms_done, 6)
            V.step(nc.vector.reciprocal(rs[:, :], rs[:, :]))
            for c in range(KT):
                ins = stt(y_[:, c, :], xt[:, c, :], vec[:, V_FIN + c:V_FIN + c + 1], rs[:, :], ALU.mult, ALU.mult)
                if c % 4 == 3:
                    ins.then_inc(s.y_out, 1)

        @block.tensor
        def _(pe):
            mm = nc.tensor.matmul

            def use(g, i=0, per=RAW, act=None, kt=0, last=KT - 1, bank=0, part=(0, 1, 2, 3), evac=None):
                n0 = g - WA0
                if part[0] == 0:
                    pe.wait_ge(raw_used, i * per + (RAW + g + 1))
                for n in part:
                    if kt == 0 and evac is not None:
                        pe.wait_ge(evac_done, evac[0] + (evac[1] + n + 1))
                    for k in range(2):
                        c = k * 512 + n * P
                        mm(ps[bank + n][:, :], whi[:, n0 % SPLIT, c:c + P], act[:, kt + k, :], start=kt + k == 0, stop=False)
                        ins = mm(ps[bank + n][:, 0:T], wlo[:, n0 % SPLIT, c:c + P], act[:, kt + k, 0:T], start=False,
                                 stop=kt + k == last)
                    ins.then_inc(quarters, 1)

            def block_of(g0, i, act, evac, per=RAW):
                for j in range(8):
                    use(g0 + j, i, per, act, 2 * j, evac=evac)

            def square_sum(use_, sq_a):
                pe.wait_ge(s.sq_sum, use_)
                mm(ps[4][:, 0:T], ones, sq_a[:, 0, :], start=True, stop=True).then_inc(s.ss_ps, 1)

            def first_block(g0, k, i, evac, sq_a, use_):
                for j in range(8):
                    if j == 4:
                        square_sum(use_, sq_a)
                    pe.wait_ge(s.acts_ready, KT * k + 2 * j + 2)
                    use(g0 + j, i, RAW, acts, 2 * j, evac=evac)

            def sum_squares(use_, buf):
                for q in range(4):
                    pe.wait_ge(s.sq_done, 4 * use_ + q + 1)
                    for c in range(4 * q, 4 * q + 4):
                        ins = mm(ps[4][:, 0:T], ones, buf[:, c, :], start=c == 0, stop=c == KT - 1)
                ins.then_inc(s.ss_ps, 1)

            pe.wait_ge(s.loaded, 48)
            sum_squares(0, scr0)
            pe.wait_ge(raw_used, RAW + WA0)
            for n in range(2 * KT):
                ins = mm(ps[5][:, n:n + 1], acc[:, n * P:(n + 1) * P], ones[:, 0:1], start=True, stop=True)
            ins.then_inc(s.mod_ps, 1)

            for j in range(8):
                pe.wait_ge(s.acts_ready, 2 * j + 2)
                use(WA0 + j, act=acts, kt=2 * j)
            with pe.Fori(1, 8) as b:
                block_of(WA0, b, acts, (b * 4, -4))
            pe.wait_ge(evac_done, 32)
            for j in range(2):
                n0 = XW0 + j - WA0
                pe.wait_ge(raw_used, RAW + XW0 + j + 1)
                for k in range(8):
                    w, c = 8 * j + k, k * P
                    mm(ps[0][:, :], whi[:, n0 % SPLIT, c:c + P], acts[:, w, :], start=w == 0, stop=False)
                    ins = mm(ps[0][:, 0:T], wlo[:, n0 % SPLIT, c:c + P], acts[:, w, 0:T], start=False, stop=w == KT - 1)
                    if k % 2:
                        ins.then_inc(quarters, 1)
            pe.wait_ge(s.gate_used, 36)
            for n in range(KT):
                ins = mm(ps[5][:, n:n + 1], gacc[:, n * P:(n + 1) * P], ones[:, 0:1], start=True, stop=True)
            ins.then_inc(s.gate_ps, 1)
            pe.wait_ge(evac_done, 33)
            pe.wait_ge(s.xz_done, 2)

            with pe.Fori(0, HT) as i:
                def weights(h):
                    use(WB0 + h // 2, i, 16, acts, h // 2 * 2 % KT, part=(0, 1) if h % 2 == 0 else (2, 3),
                        evac=(i * 8, 29 + h // 16 * 4))

                pe.wait_ge(s.lora_ready, i + 1)
                mm(ps[4][:, :], lw[:, :], xz[:, :], start=True, stop=True).then_inc(s.z_ps, 1)
                weights(0)
                weights(1)
                pe.wait_ge(s.sq_ready, i + 1)
                mm(ps[5][:, 0:T], blk, t2[:, :], start=True, stop=True).then_inc(s.ss2_ps, 1)
                weights(2)
                weights(3)
                pe.wait_ge(s.br_ready, i + 1)
                mm(ps[5][:, T:2 * T], blk, t1[:, :], start=True, stop=True).then_inc(s.bs_ps, 1)
                weights(4)
                weights(5)
                pe.wait_ge(s.ops_done, i * 8 + 8)

                def pairs(c, bank):
                    mm(ps[bank][:, 0:T], bx[:, c, :], ar[:, c, :], start=True, stop=True)
                    mm(ps[bank][:, T:2 * T], kx[:, c, :], ar[:, c, :], start=True, stop=True).then_inc(s.g_ps, 1)

                pairs(0, 6)
                pairs(1, 7)
                weights(6)
                pe.wait_ge(s.bon_done, i + 1)
                pairs(2, 4)
                pairs(3, 5)
                weights(7)
                weights(8)

                def transposes(src, bank, sem_):
                    for c in range(NC):
                        ins = nc.tensor.transpose(four(bank)[:, c, :], src[:, c, 0:P], ident)
                    ins.then_inc(sem_, 1)

                pe.wait_ge(s.mt_upd, i * 6 + 1)
                transposes(mt, 6, s.m_ps)
                transposes(ar, 7, s.tr_ps)
                pe.wait_ge(s.vx_done, i * 2 + 2)
                transposes(vx, 4, s.tr_ps)
                weights(9)
                weights(10)
                for n in range(1, 6):
                    pe.wait_ge(s.lt_ready, i * 5 + n)
                    pe.wait_ge(s.m_first, i + 1) if n == 1 else pe.wait_ge(s.m_upd, i * 4 + (n - 1))
                    for c in range(NC):
                        ins = mm(four(6)[:, c, :], lt[:, c, :], mi[:, c, :], start=True, stop=True)
                    ins.then_inc(s.t_ps, 1)
                    if n == 1:
                        pe.wait_ge(s.bk_scaled, i * 2 + 2)
                        transposes(bx, 5, s.tr_ps)
                    if n == 2:
                        pe.wait_ge(s.tr_done, i * 4 + 3)
                        transposes(kx, 5, s.tr_ps)
                    weights(9 + 2 * n)
                    pe.wait_ge(s.t_done, i * 5 + n)
                    pe.wait_ge(s.mt_upd, i * 6 + n)
                    if n == 1:
                        pe.wait_ge(s.tr_done, i * 4 + 2)
                    if n < 5:
                        for c in range(NC):
                            ins = mm(four(7)[:, c, :], mt[:, c, :], ts[:, c, :], start=True, stop=True)
                        ins.then_inc(s.u_ps, 1)
                    for c in range(NC):
                        ins = mm(four(4)[:, c, :], ts[:, c, :], mt[:, c, :], start=True, stop=True)
                    ins.then_inc(s.ut_ps, 1)
                    weights(10 + 2 * n)
                for c in range(NC):
                    ins = mm(four(7)[:, c, :], gm[:, c, T:T + P], vx[:, c, :], start=True, stop=True)
                ins.then_inc(s.x_ps, 1)
                pe.wait_ge(s.mt_upd, i * 6 + 6)
                for c in range(NC):
                    ins = mm(four(6)[:, c, :], ar[:, c, 0:P], mt[:, c, :], start=True, stop=True)
                ins.then_inc(s.w_ps, 1)
                weights(21)
                pe.wait_ge(s.x_done, i + 1)
                for c in range(NC):
                    ins = mm(four(5)[:, c, :], mt[:, c, :], ts[:, c, :], start=True, stop=True)
                ins.then_inc(s.u2_ps, 1)
                weights(22)
                pe.wait_ge(s.u2_done, i + 1)

                def add(c, sa_c):
                    mm(ps[7][:, 0:P], bx[:, c, :], sa_c, start=True, stop=False)
                    mm(ps[7][:, 0:P], kx[:, c, :], vx[:, c, :], start=False, stop=True).then_inc(s.d_ps, 1)

                def outputs(c, sa_c):
                    y = four(4)[:, c, :]
                    mm(y, vx[:, c, :], gm[:, c, T + P:T + 2 * P], start=True, stop=False)
                    if c:
                        mm(y, st[:, 1 - c % 2, :], ar[:, c, P:2 * P], start=False, stop=False)
                    return mm(y, sa_c, gm[:, c, P:2 * P], start=False, stop=True)

                add(0, lt[:, 0, :])
                outputs(0, lt[:, 0, :])
                weights(23)
                for c in range(1, NC):
                    pe.wait_ge(s.s_done, i * 3 + c)
                    mm(ps[6][:, 0:P], mi[:, c, :], st[:, 1 - c % 2, :], start=True, stop=True).then_inc(s.sa_ps, 1)
                    weights(22 + 2 * c)
                    pe.wait_ge(s.sa_done, i * 3 + c)
                    if c < NC - 1:
                        add(c, sa[:, c % 2, :])
                    ins = outputs(c, sa[:, c % 2, :])
                    if c < NC - 1:
                        weights(23 + 2 * c)
                ins.then_inc(s.y_ps, 1)
                pe.wait_ge(s.yc_done, i * 2 + 2)
                mm(ps[5][:, 0:T], blkm, t1[:, :], start=True, stop=True).then_inc(s.mu_ps, 1)
                weights(29)
                pe.wait_ge(s.ysq_done, i + 1)
                mm(ps[5][:, T:2 * T], blkm, t2[:, :], start=True, stop=True).then_inc(s.var_ps, 1)
                weights(30)
                weights(31)

            pe.wait_ge(evac_done, 33 + 8 * HT)
            E = 33 + 8 * HT
            for b in range(4):
                for j in range(8):
                    if b == 0:
                        pe.wait_ge(s.yab_done, 2 * j + 2)
                    use(PAB0 + 8 * b + j, act=yab[:, j // 4, :, :], kt=2 * j % 8, last=7, bank=j // 4 * 4,
                        evac=(E + 8 * b + j // 4 * 4, -8) if b else None)
            E += 32
            for j in range(8):
                pe.wait_ge(s.m_done, 2 * j + 2)
                use(WO0 + j, act=acts, kt=2 * j, evac=(E - 4, 0))
            with pe.Fori(1, 4) as b:
                block_of(WO0, b, acts, (b * 4, E - 4))
            E += 16
            square_sum(1, sqa)
            first_block(NS0, 1, 0, (E - 4, 0), sqb, 2)
            with pe.Fori(1, NG) as b:
                block_of(NS0, b, acts, (b * 4, E - 4))
            E += 4 * NG
            pe.wait_ge(s.rs_ready, 1)
            for q in range(2):
                ins = nc.tensor.transpose(ps[6][:, q * P:(q + 1) * P], rs[:, q * P:(q + 1) * P], ident)
            ins.then_inc(s.rst_ps, 1)
            n0 = (GT0 - WA0) % SPLIT
            pe.wait_ge(raw_used, RAW + GT0 + 1)
            for k in range(KT):
                hi_w, lo_w = (w[:, n0, k * GCOL:(k + 1) * GCOL] for w in (whi, wlo))
                for q in range(2):
                    dst = ps[4 + q][:, 0:GCOL]
                    mm(dst, acts[:, k, q * P:(q + 1) * P], hi_w, start=k == 0, stop=False)
                    mm(dst, acts[:, k, q * P:(q + 1) * P], lo_w, start=False, stop=False)
                    ins = mm(dst, acts[:, k, T + q * P:T + (q + 1) * P], hi_w, start=False, stop=k == KT - 1)
                if k % 4 == 3:
                    ins.then_inc(quarters, 1)
            NB = GQ * NCMP
            for x in range(2):
                pe.wait_ge(s.blk_lo, x + 1)
                for j in range(4):
                    n0 = CM0 + 4 * x + j - WA0
                    pe.wait_ge(raw_used, RAW + n0 + WA0 + 1)
                    for k in range(8):
                        l = 8 * j + k
                        c = k * P
                        mm(ps[6 + x][:, 0:2 * NB], whi[:, n0 % SPLIT, c:c + P], blks[:, l, :], start=l == 0, stop=False)
                        ins = mm(ps[6 + x][:, 0:NB], wlo[:, n0 % SPLIT, c:c + P], blks[:, l, 0:NB], start=False, stop=l == CL - 1)
                        if k % 2:
                            ins.then_inc(quarters, 1)
            pe.wait_ge(s.cmp2_in, 16)
            pe.wait_ge(s.blk_done, 4)
            pe.wait_ge(s.gt_done, 2)
            mm(ps[4][:, 0:NB], cmp2[:, 0:P], hid[:, 0, :], start=True, stop=True).then_inc(s.cmp_ps, 1)
            pe.wait_ge(s.hrep_done, GQ)
            for g in range(GQ):
                ins = mm(four(5)[:, g, :], hrep[:, g, :], cmp2[:, P:2 * P], start=True, stop=True)
            ins.then_inc(s.cmp_ps, 1)
            pe.wait_ge(s.kcmp_done, 1)
            pe.wait_ge(s.vcmp_done, 1)
            pe.wait_ge(s.scaled, 4 * NG)
            with pe.Fori(0, GQ) as g:
                pe.wait_ge(s.ng_done, g + 1)
                pe.wait_ge(s.ng_dve, g * 3 + 3)
                for j in range(HPG):
                    qT = ng[:, j, P:2 * P]
                    mm(ps[j][:, 0:T], qT, ng[:, G_KS, :], start=True, stop=True)
                    ins = mm(ps[j][:, T:2 * T], qT, ng[:, G_KW, :], start=True, stop=True)
                ins.then_inc(s.s_ps, 1)
                pe.wait_ge(s.attn_done, g * 2 + 1)
                for j in range(HPG):
                    qT = ng[:, j, 0:P]
                    for x in range(2):
                        c = (j % 2 * 2 + x) * P
                        ins = mm(ps[5 + j // 2][:, c:c + P], qT, ng[:, (G_KS, G_KW)[x], 0:P], start=True, stop=True)
                ins.then_inc(s.s_ps, 1)
                for j in range(HPG):
                    for q in (1, 0):
                        c = (1 - q) * P + j * NP32
                        ins = mm(ps[4][:, c:c + NP32], ng[:, j, q * P:(q + 1) * P], kcg[:, :], start=True, stop=True)
                ins.then_inc(s.s_ps, 1)
                for n in range(4):
                    ins = nc.tensor.transpose(four(7)[:, n, :], ng[:, (G_VS, G_VW)[n // 2], n % 2 * P:(n % 2 + 1) * P], ident)
                ins.then_inc(s.v_ps, 1)
                for q in (1, 0):
                    pe.wait_ge(s.pr_done, g * 18 + (9 if q else 18))
                    if q:
                        for n in range(4):
                            for j in range(HPG):
                                ins = nc.tensor.transpose(four(n)[:, j, :], pr1[:, j, n * P:(n + 1) * P], ident)
                            ins.then_inc(s.p_ps, 1)
                    else:
                        for n in range(2):
                            for j in range(HPG):
                                ins = nc.tensor.transpose(four(5 + n)[:, j, :], pr0[:, j, n * P:(n + 1) * P], ident)
                            ins.then_inc(s.p_ps, 1)
                    t = 1 - q
                    nc.tensor.transpose(ps[4][:, t * P:(t + 1) * P], pc[:, t * HPG:(t + 1) * HPG, :].rearrange("p h n -> p (h n)"),
                                        ident).then_inc(s.p_ps, 1)
                    pe.wait_ge(s.pt_act, g * 11 + (6 if q else 11))
                    pe.wait_ge(s.pt_dve, g * 3 + (2 if q else 3))
                    if q:
                        pe.wait_ge(s.vtm_done, g + 1)
                    dst = ps[7 if q else 4][:, :]
                    for n in range(4 if q else 2):
                        v = vtm[:, n if q else 2 * n, :]
                        mm(dst, v, pt[:, n, :], start=n == 0, stop=False)
                    mm(dst, vcg[:, :], pt[:, 4, :], start=False, stop=True).then_inc(s.o_ps, 1)
            pe.wait_ge(s.attn_done, 2 * GQ + 1)
            with pe.Fori(0, 4) as b:
                block_of(NO0, b, acts, (b * 4, E - 4))
            E += KT

            def ffn(f, first):
                if first:
                    first_block(FF0, 2, 0, (E - 4, 0), sqb, 3)
                with pe.Fori(1 if first else 0, 4) as b:
                    block_of(FF0, f * 8 + b, acts, (f * 32 + b * 4, E - 4))
                for j in range(8):
                    pe.wait_ge(s.relu_lo, f * 16 + (2 * j + 2))
                    use(FF0 + 32 + j, f * 8, RAW, hff, 2 * j, evac=(f * 32, E + 12))
                with pe.Fori(1, 4) as b:
                    block_of(FF0 + 32, f * 8 + b, hff, (f * 32 + b * 4, E + 12))

            ffn(0, True)
            with pe.Fori(1, 4) as f:
                ffn(f, False)
            E += 128
            pe.wait_ge(s.pes_lo, 1)
            for b in range(4):
                use(PR0 + b, act=pes, last=1, evac=(E + 4 * b, -4))
            E += KT
            first_block(PG0, 3, 0, (E - 4, 0), sqb, 4)
            with pe.Fori(1, 4) as b:
                block_of(PG0, b, acts, (b * 4, E - 4))
            square_sum(5, sqb)


def kernel(**inputs):
    import concourse.bacc as bacc
    from concourse.bass_utils import run_bass_kernel_spmd

    nc = bacc.Bacc("TRN2", target_bir_lowering=False, num_devices=1)
    arrays, args = {}, []
    for name, a in lay_out({k: np.asarray(v) for k, v in inputs.items()}).items():
        a = np.ascontiguousarray(a)
        arrays[f"in_{name}"] = a
        args.append(nc.dram_tensor(f"in_{name}", a.shape, mybir.dt.from_np(a.dtype), kind="ExternalInput").ap())
    out = nc.dram_tensor("out", (P, KT, T), F32, kind="ExternalOutput").ap()
    block_of_two_layers(nc, *args, out)
    r = run_bass_kernel_spmd(nc, [arrays], core_ids=[0])
    y = r.results[0]["out"]
    return y.transpose(2, 1, 0).reshape(1, T, D)
```
